# Optimizing a Trainium2 kernel written in Bass

```python
import math
import jax, jax.numpy as jnp
from jax import lax
import numpy as np
import jax
import jax.numpy as jnp

D_MODEL = 1024
BATCH = 1
SEQ = 256
DEPTH = 4

CHUNK = 64
N_MIXERS = 3
EPS = 1e-6
N_FOX = (DEPTH + 2) // 3
N_S5 = (DEPTH + 1) // 3
N_POOL = DEPTH // 3
FOX_HEADS = 16
FOX_HEAD_DIM = D_MODEL // FOX_HEADS
Q_BLOCK = 128
FOX_IN = 3 * D_MODEL + FOX_HEADS
FORGET_BIAS_CENTER = 3.0
S5_GROUP = 16
S5_GROUPS = D_MODEL // S5_GROUP
S5_STATE = 64
S5_DT_MIN = 1e-3
S5_DT_MAX = 1e-1
POOL_WINDOWS = (2, 4, 8, 16)
POOL_GROUPS = len(POOL_WINDOWS)
POOL_WIDTH = D_MODEL // POOL_GROUPS
D_FF = -(-8 * D_MODEL // (3 * 256)) * 256


F32 = jnp.float32

def rms_norm(x, g):
    xf = x.astype(F32)
    y = xf * lax.rsqrt(jnp.mean(xf * xf, axis=-1, keepdims=True) + EPS)
    return (y * g.astype(F32)).astype(x.dtype)

def forgetting_attention(h, w_in, b_f, w_out):
    B, S, _ = h.shape
    proj = h @ w_in
    q, k, v, f_logit = jnp.split(proj, [D_MODEL, 2 * D_MODEL, 3 * D_MODEL], axis=-1)

    def heads(t):
        return t.reshape(B, S, FOX_HEADS, FOX_HEAD_DIM).transpose(0, 2, 1, 3).astype(F32)

    q, k, v = heads(q), heads(k), heads(v)
    log_f = jax.nn.log_sigmoid(f_logit.astype(F32) + b_f.astype(F32))
    c = jnp.cumsum(log_f, axis=1).transpose(0, 2, 1)
    n_blk = S // Q_BLOCK
    q_blocks = q.reshape(B, FOX_HEADS, n_blk, Q_BLOCK, FOX_HEAD_DIM).transpose(2, 0, 1, 3, 4)
    c_blocks = c.reshape(B, FOX_HEADS, n_blk, Q_BLOCK).transpose(2, 0, 1, 3)
    starts = jnp.arange(n_blk, dtype=jnp.int32) * Q_BLOCK
    key_pos = jnp.arange(S, dtype=jnp.int32)
    scale = FOX_HEAD_DIM ** -0.5

    def one_block(args):
        q_b, c_b, start = args
        logits = jnp.einsum('bhqd,bhkd->bhqk', q_b, k) * scale
        logits = logits + c_b[..., :, None] - c[..., None, :]
        q_pos = start + jnp.arange(Q_BLOCK, dtype=jnp.int32)
        mask = key_pos[None, :] <= q_pos[:, None]
        p = jax.nn.softmax(jnp.where(mask, logits, -jnp.inf), axis=-1)
        return jnp.einsum('bhqk,bhkd->bhqd', p, v)

    out = lax.map(one_block, (q_blocks, c_blocks, starts))
    out = out.transpose(1, 0, 3, 2, 4).reshape(B, S, D_MODEL).astype(h.dtype)
    return out @ w_out

def s5_layer(h, w_in, a_re, a_im, log_dt, b_re, b_im, c_re, c_im, d, w_glu):
    B, S, _ = h.shape
    u = (h @ w_in).astype(F32)
    u_g = u.reshape(B, S, S5_GROUPS, S5_GROUP).astype(jnp.complex64)
    lam = lax.complex(a_re.astype(F32), a_im.astype(F32))
    dt = jnp.exp(log_dt.astype(F32))[:, None]
    lam_bar = jnp.exp(lam * dt)
    b_mat = lax.complex(b_re.astype(F32), b_im.astype(F32))
    b_bar = ((lam_bar - 1.0) / lam)[..., None] * b_mat
    bu = jnp.einsum('gpc,bsgc->bsgp', b_bar, u_g)
    lam_seq = jnp.broadcast_to(lam_bar, bu.shape)

    def combine(left, right):
        a_l, s_l = left
        a_r, s_r = right
        return a_r * a_l, a_r * s_l + s_r

    _, states = lax.associative_scan(combine, (lam_seq, bu), axis=1)
    c_mat = lax.complex(c_re.astype(F32), c_im.astype(F32))
    y = jnp.einsum('gcp,bsgp->bsgc', c_mat, states).real.reshape(B, S, D_MODEL)
    y = y + d.astype(F32) * u
    g = jax.nn.gelu(y).astype(h.dtype)
    val, gate = jnp.split(g @ w_glu, 2, axis=-1)
    return val * jax.nn.sigmoid(gate)

def multiscale_pool(h, w_grp, b_grp, scale):
    B, S, _ = h.shape
    hf = h.astype(F32).reshape(B, S, POOL_GROUPS, POOL_WIDTH)
    count_base = jnp.arange(1, S + 1, dtype=F32)[None, :, None]
    outs = []
    for gi, w in enumerate(POOL_WINDOWS):
        xg = hf[:, :, gi]
        cs = jnp.cumsum(xg, axis=1)
        lag = jnp.pad(cs[:, :-w], ((0, 0), (w, 0), (0, 0)))
        mean = (cs - lag) / jnp.minimum(count_base, float(w))
        outs.append(jnp.einsum('bsc,cd->bsd', mean - xg, w_grp[gi].astype(F32)))
    y = jnp.concatenate(outs, axis=-1) + b_grp.astype(F32)
    return (y * scale.astype(F32)).astype(h.dtype)

def swiglu(h, w_gate_up, w_down):
    g, u = jnp.split(h @ w_gate_up, 2, axis=-1)
    return (jax.nn.silu(g) * u) @ w_down

def first_inputs(seed: int = 0) -> dict:
    key = jax.random.key(seed)
    ks = jax.random.split(key, 24)
    D, H, G, P, C = D_MODEL, FOX_HEADS, S5_GROUPS, S5_STATE, S5_GROUP
    nrm = jax.random.normal
    x = nrm(ks[0], (BATCH, SEQ, D), F32)
    mix_norm_g = 1.0 + 0.05 * nrm(ks[1], (DEPTH, D), F32)
    ffn_norm_g = 1.0 + 0.05 * nrm(ks[2], (DEPTH, D), F32)
    final_norm_g = 1.0 + 0.05 * nrm(ks[3], (D,), F32)
    fox_w_in = nrm(ks[4], (N_FOX, D, FOX_IN), F32) * D ** -0.5
    fox_b_f = FORGET_BIAS_CENTER + 0.5 * nrm(ks[5], (N_FOX, H), F32)
    fox_w_out = nrm(ks[6], (N_FOX, D, D), F32) * D ** -0.5
    s5_w_in = nrm(ks[7], (N_S5, D, D), F32) * D ** -0.5
    s5_a_re = -0.5 + 0.01 * nrm(ks[8], (N_S5, G, P), F32)
    s5_a_im = math.pi * jnp.arange(P, dtype=F32)[None, None, :] + 0.01 * nrm(ks[9], (N_S5, G, P), F32)
    s5_log_dt = jax.random.uniform(ks[10], (N_S5, G), F32, math.log(S5_DT_MIN), math.log(S5_DT_MAX))
    s5_b_re = nrm(ks[11], (N_S5, G, P, C), F32) * (2 * C) ** -0.5
    s5_b_im = nrm(ks[12], (N_S5, G, P, C), F32) * (2 * C) ** -0.5
    s5_c_re = nrm(ks[13], (N_S5, G, C, P), F32) * P ** -0.5
    s5_c_im = nrm(ks[14], (N_S5, G, C, P), F32) * P ** -0.5
    s5_d = nrm(ks[15], (N_S5, D), F32)
    s5_w_glu = nrm(ks[16], (N_S5, D, 2 * D), F32) * D ** -0.5
    pool_w = nrm(ks[17], (N_POOL, POOL_GROUPS, POOL_WIDTH, POOL_WIDTH), F32) * POOL_WIDTH ** -0.5
    pool_b = 0.01 * nrm(ks[18], (N_POOL, D), F32)
    pool_scale = 0.5 + 0.05 * nrm(ks[19], (N_POOL, D), F32)
    ffn_w_gate_up = nrm(ks[20], (DEPTH, D, 2 * D_FF), F32) * D ** -0.5
    ffn_w_down = nrm(ks[21], (DEPTH, D_FF, D), F32) * D_FF ** -0.5
    return {"x": x, "mix_norm_g": mix_norm_g, "ffn_norm_g": ffn_norm_g, "final_norm_g": final_norm_g,
            "fox_w_in": fox_w_in, "fox_b_f": fox_b_f, "fox_w_out": fox_w_out,
            "s5_w_in": s5_w_in, "s5_a_re": s5_a_re, "s5_a_im": s5_a_im, "s5_log_dt": s5_log_dt,
            "s5_b_re": s5_b_re, "s5_b_im": s5_b_im, "s5_c_re": s5_c_re, "s5_c_im": s5_c_im,
            "s5_d": s5_d, "s5_w_glu": s5_w_glu,
            "pool_w": pool_w, "pool_b": pool_b, "pool_scale": pool_scale,
            "ffn_w_gate_up": ffn_w_gate_up, "ffn_w_down": ffn_w_down}

def first_block(x, mix_norm_g, ffn_norm_g, final_norm_g, fox_w_in, fox_b_f, fox_w_out,
              s5_w_in, s5_a_re, s5_a_im, s5_log_dt, s5_b_re, s5_b_im, s5_c_re, s5_c_im,
              s5_d, s5_w_glu, pool_w, pool_b, pool_scale, ffn_w_gate_up, ffn_w_down):
    for i in range(DEPTH):
        h = rms_norm(x, mix_norm_g[i])
        kind, j = i % N_MIXERS, i // N_MIXERS
        if kind == 0:
            mix = forgetting_attention(h, fox_w_in[j], fox_b_f[j], fox_w_out[j])
        elif kind == 1:
            mix = s5_layer(h, s5_w_in[j], s5_a_re[j], s5_a_im[j], s5_log_dt[j], s5_b_re[j], s5_b_im[j],
                           s5_c_re[j], s5_c_im[j], s5_d[j], s5_w_glu[j])
        else:
            mix = multiscale_pool(h, pool_w[j], pool_b[j], pool_scale[j])
        x = x + mix.astype(x.dtype)
        x = x + swiglu(rms_norm(x, ffn_norm_g[i]), ffn_w_gate_up[i], ffn_w_down[i]).astype(x.dtype)
    return rms_norm(x, final_norm_g)


DEPTH_2 = 2

ROPE_BASE = 10000.0
LN_EPS = 1e-5
NEG = -1e30

RET_HEADS = 4
RET_DIM = 64
RET_W = RET_HEADS * RET_DIM
MLA_HEADS = 8
MLA_NOPE = 64
MLA_ROPE = 32
MLA_V = 64
MLA_Q_RANK = 256
MLA_KV_RANK = 128
MLA_W = MLA_HEADS * MLA_V
MLSTM_HEADS = 4
MLSTM_DIM = 64
MLSTM_W = MLSTM_HEADS * MLSTM_DIM
MLSTM_CONV = 4
MIX_W = RET_W + MLA_W + MLSTM_W

IN_SIZES = (RET_W, RET_W, RET_W, RET_W, MLA_Q_RANK, MLA_KV_RANK, MLA_ROPE, MLSTM_W, MLSTM_W, MLSTM_W, MLSTM_W, MLSTM_HEADS, MLSTM_HEADS)
IN_IS_VALUE = (False, False, True, False, False, False, False, False, False, True, False, False, False)
D_IN = sum(IN_SIZES)

D_FF_2 = 2816
N_EXPERTS = 8
TOP_K = 2
D_FF_EXPERT = 3584
N_DENSE = (DEPTH_2 + 1) // 2
N_MOE = DEPTH_2 // 2

DN_ALPHA = (2 * DEPTH_2) ** 0.25
DN_BETA = (8 * DEPTH_2) ** -0.25


def layer_norm(x, w, b):
    x32 = x.astype(jnp.float32)
    mu = x32.mean(-1, keepdims=True)
    var = jnp.square(x32 - mu).mean(-1, keepdims=True)
    return ((x32 - mu) * lax.rsqrt(var + LN_EPS) * w + b).astype(x.dtype)

def rms_norm_2(x, w):
    x32 = x.astype(jnp.float32)
    y = x32 * lax.rsqrt(jnp.square(x32).mean(-1, keepdims=True) + LN_EPS) * w
    return y.astype(x.dtype)

def head_norm(x, w, n_heads):
    b, s, wd = x.shape
    xh = x.astype(jnp.float32).reshape(b, s, n_heads, wd // n_heads)
    mu = xh.mean(-1, keepdims=True)
    var = jnp.square(xh - mu).mean(-1, keepdims=True)
    return ((xh - mu) * lax.rsqrt(var + LN_EPS)).reshape(b, s, wd) * w

def to_heads(x, n):
    b, s, w = x.shape
    return x.reshape(b, s, n, w // n).transpose(0, 2, 1, 3)

def from_heads(x):
    b, h, s, d = x.shape
    return x.transpose(0, 2, 1, 3).reshape(b, s, h * d)

def rope(x, pos):
    half = x.shape[-1] // 2
    inv = ROPE_BASE ** (-jnp.arange(half, dtype=jnp.float32) / half)
    ang = pos[:, None] * inv[None, :]
    cos, sin = jnp.cos(ang), jnp.sin(ang)
    x32 = x.astype(jnp.float32)
    x1, x2 = x32[..., :half], x32[..., half:]
    return jnp.concatenate([x1 * cos - x2 * sin, x1 * sin + x2 * cos], -1).astype(x.dtype)

def retention(q, k, v):
    b, h, s, d = q.shape
    L = CHUNK
    nc = s // L
    log_gamma = jnp.log(1.0 - 2.0 ** (-5.0 - jnp.arange(h, dtype=jnp.float32)))
    idx = jnp.arange(L, dtype=jnp.float32)
    diff = idx[:, None] - idx[None, :]
    inner_decay = jnp.where(diff >= 0, jnp.exp(diff[None] * log_gamma[:, None, None]), 0.0)
    qc = q.astype(jnp.float32).reshape(b, h, nc, L, d)
    kc = (k.astype(jnp.float32) * d ** -0.5).reshape(b, h, nc, L, d)
    vc = v.astype(jnp.float32).reshape(b, h, nc, L, d)
    scores = jnp.einsum('bhcld,bhcmd->bhclm', qc, kc) * inner_decay[None, :, None]
    inner = jnp.einsum('bhclm,bhcme->bhcle', scores, vc)
    kv_w = jnp.exp((L - 1 - idx)[None, :] * log_gamma[:, None])
    local = jnp.einsum('bhcmd,bhcme->bhcde', kc * kv_w[None, :, None, :, None], vc)
    chunk_decay = jnp.exp(L * log_gamma)[None, :, None, None]

    def step(state, loc):
        return chunk_decay * state + loc, state

    _, r_prev = lax.scan(step, jnp.zeros((b, h, d, d), jnp.float32), jnp.moveaxis(local, 2, 0))
    r_prev = jnp.moveaxis(r_prev, 0, 2)
    q_w = jnp.exp((idx + 1.0)[None, :] * log_gamma[:, None])
    cross = jnp.einsum('bhcld,bhcde->bhcle', qc, r_prev) * q_w[None, :, None, :, None]
    return (inner + cross).reshape(b, h, s, d)

def mlstm(q, k, v, ig, fg):
    b, h, s, d = q.shape
    L = CHUNK
    nc = s // L
    qc = q.astype(jnp.float32).reshape(b, h, nc, L, d)
    kc = (k.astype(jnp.float32) * d ** -0.5).reshape(b, h, nc, L, d)
    vc = v.astype(jnp.float32).reshape(b, h, nc, L, d)
    ic = ig.astype(jnp.float32).reshape(b, h, nc, L)
    lf = jax.nn.log_sigmoid(fg.astype(jnp.float32)).reshape(b, h, nc, L)
    bcum = jnp.cumsum(lf, axis=-1)
    g = bcum[..., -1]
    a = g[..., None] - bcum + ic
    amax = a.max(-1)
    wa = jnp.exp(a - amax[..., None])
    loc_c = jnp.einsum('bhcl,bhcld,bhcle->bhcde', wa, kc, vc)
    loc_n = jnp.einsum('bhcl,bhcld->bhcd', wa, kc)

    def step(carry, xs):
        c_s, n_s, m_s = carry
        g_c, amax_c, lc, ln = xs
        m_new = jnp.maximum(g_c + m_s, amax_c)
        sp = jnp.exp(g_c + m_s - m_new)
        sl = jnp.exp(amax_c - m_new)
        c_new = sp[..., None, None] * c_s + sl[..., None, None] * lc
        n_new = sp[..., None] * n_s + sl[..., None] * ln
        return (c_new, n_new, m_new), (c_s, n_s, m_s)

    init = (jnp.zeros((b, h, d, d), jnp.float32), jnp.zeros((b, h, d), jnp.float32), jnp.full((b, h), NEG, jnp.float32))
    xs = (jnp.moveaxis(g, 2, 0), jnp.moveaxis(amax, 2, 0), jnp.moveaxis(loc_c, 2, 0), jnp.moveaxis(loc_n, 2, 0))
    _, (c_prev, n_prev, m_prev) = lax.scan(step, init, xs)
    c_prev = jnp.moveaxis(c_prev, 0, 2)
    n_prev = jnp.moveaxis(n_prev, 0, 2)
    m_prev = jnp.moveaxis(m_prev, 0, 2)
    idx = jnp.arange(L)
    causal = idx[:, None] >= idx[None, :]
    log_d = jnp.where(causal, bcum[..., :, None] - bcum[..., None, :] + ic[..., None, :], NEG)
    inter = bcum + m_prev[..., None]
    m_t = jnp.maximum(inter, log_d.max(-1))
    dw = jnp.exp(log_d - m_t[..., None])
    cmat = jnp.einsum('bhcld,bhcmd->bhclm', qc, kc) * dw
    si = jnp.exp(inter - m_t)
    num = jnp.einsum('bhclm,bhcme->bhcle', cmat, vc) + si[..., None] * jnp.einsum('bhcld,bhcde->bhcle', qc, c_prev)
    den = cmat.sum(-1) + si * jnp.einsum('bhcld,bhcd->bhcl', qc, n_prev)
    hcell = num / jnp.maximum(jnp.abs(den), jnp.exp(-m_t))[..., None]
    return hcell.reshape(b, h, s, d)

def mla_attention(q_nope, q_rope, k_nope, k_rope, v):
    b, h, s, dn = q_nope.shape
    dr = q_rope.shape[-1]
    nq = s // Q_BLOCK
    scale = (dn + dr) ** -0.5
    kpos = jnp.arange(s)
    qn_b = q_nope.reshape(b, h, nq, Q_BLOCK, dn).transpose(2, 0, 1, 3, 4)
    qr_b = q_rope.reshape(b, h, nq, Q_BLOCK, dr).transpose(2, 0, 1, 3, 4)

    def block(args):
        qn, qr, i = args
        sc = jnp.einsum('bhqd,bhkd->bhqk', qn, k_nope) + jnp.einsum('bhqr,bkr->bhqk', qr, k_rope)
        sc = sc.astype(jnp.float32) * scale
        qpos = i * Q_BLOCK + jnp.arange(Q_BLOCK)
        limit = (qpos // CHUNK + 1) * CHUNK
        sc = jnp.where(kpos[None, :] < limit[:, None], sc, NEG)
        p = jax.nn.softmax(sc, axis=-1).astype(v.dtype)
        return jnp.einsum('bhqk,bhkd->bhqd', p, v)

    out = lax.map(block, (qn_b, qr_b, jnp.arange(nq)))
    return out.transpose(1, 2, 0, 3, 4).reshape(b, h, s, v.shape[-1])

def causal_dwconv(x, w, bias):
    kw, c = w.shape
    y = lax.conv_general_dilated(x, w.reshape(kw, 1, c).astype(x.dtype), window_strides=(1,), padding=[(kw - 1, 0)], dimension_numbers=('NWC', 'WIO', 'NWC'), feature_group_count=c)
    return y + bias

def hybrid_mixer(x, pos, w_in, ret_gn_w, mla_q_norm_w, mla_w_uq, mla_kv_norm_w, mla_w_ukv, conv_w, conv_b, b_i, b_f, mlstm_gn_w, w_out):
    bsz, s, _ = x.shape
    hcat = x @ w_in
    offsets = np.cumsum(IN_SIZES)[:-1].tolist()
    (r_q, r_k, r_v, r_g, c_q, c_kv, k_r, m_q, m_k, m_v, m_o, m_i, m_f) = jnp.split(hcat, offsets, axis=-1)
    rq = rope(to_heads(r_q, RET_HEADS), pos)
    rk = rope(to_heads(r_k, RET_HEADS), pos)
    ret = retention(rq, rk, to_heads(r_v, RET_HEADS))
    ret_out = jax.nn.silu(r_g.astype(jnp.float32)) * head_norm(from_heads(ret), ret_gn_w, RET_HEADS)
    qf = (rms_norm_2(c_q, mla_q_norm_w) @ mla_w_uq).reshape(bsz, s, MLA_HEADS, MLA_NOPE + MLA_ROPE).transpose(0, 2, 1, 3)
    q_nope, q_rope = qf[..., :MLA_NOPE], rope(qf[..., MLA_NOPE:], pos)
    kvf = (rms_norm_2(c_kv, mla_kv_norm_w) @ mla_w_ukv).reshape(bsz, s, MLA_HEADS, MLA_NOPE + MLA_V).transpose(0, 2, 1, 3)
    k_nope, v_mla = kvf[..., :MLA_NOPE], kvf[..., MLA_NOPE:]
    k_rope = rope(k_r, pos)
    att_out = from_heads(mla_attention(q_nope, q_rope, k_nope, k_rope, v_mla))
    qk = jax.nn.silu(causal_dwconv(jnp.concatenate([m_q, m_k], -1), conv_w, conv_b))
    mq, mk = qk[..., :MLSTM_W], qk[..., MLSTM_W:]
    ig = (m_i + b_i).transpose(0, 2, 1)
    fg = (m_f + b_f).transpose(0, 2, 1)
    hcell = mlstm(to_heads(mq, MLSTM_HEADS), to_heads(mk, MLSTM_HEADS), to_heads(m_v, MLSTM_HEADS), ig, fg)
    h_gated = jax.nn.sigmoid(m_o.astype(jnp.float32)) * from_heads(hcell)
    mlstm_out = head_norm(h_gated, mlstm_gn_w, MLSTM_HEADS)
    merged = jnp.concatenate([ret_out.astype(x.dtype), att_out.astype(x.dtype), mlstm_out.astype(x.dtype)], -1)
    return merged @ w_out

def swiglu_2(x, wg, wu, wd):
    return (jax.nn.silu(x @ wg) * (x @ wu)) @ wd

def moe_swiglu(x, router, wg, wu, wd):
    bsz, s, d = x.shape
    t = x.reshape(bsz * s, d)
    logits = (t @ router).astype(jnp.float32)
    top_v, top_i = lax.top_k(logits, TOP_K)
    top_w = jax.nn.softmax(top_v, axis=-1)
    gate = jnp.sum(jax.nn.one_hot(top_i, N_EXPERTS, dtype=jnp.float32) * top_w[..., None], axis=1)
    y = jnp.zeros((bsz * s, d), jnp.float32)
    for e in range(N_EXPERTS):
        y = y + gate[:, e:e + 1] * swiglu_2(t, wg[e], wu[e], wd[e]).astype(jnp.float32)
    return y.astype(x.dtype).reshape(bsz, s, d)

def second_inputs(seed: int = 0) -> dict:
    key = jax.random.key(seed)
    ks = jax.random.split(key, 24)
    L = DEPTH_2

    def nrm(k, shape, scale):
        return jax.random.normal(k, shape, jnp.float32) * scale

    col_scale = np.concatenate([np.full(n, DN_BETA if isv else 1.0, np.float32) for n, isv in zip(IN_SIZES, IN_IS_VALUE)])
    ukv_scale = np.tile(np.concatenate([np.ones(MLA_NOPE, np.float32), np.full(MLA_V, DN_BETA, np.float32)]), MLA_HEADS)
    return {
        'x': nrm(ks[0], (BATCH, SEQ, D_MODEL), 1.0),
        'w_in': nrm(ks[1], (L, D_MODEL, D_IN), D_MODEL ** -0.5) * jnp.asarray(col_scale),
        'ret_gn_w': 1.0 + nrm(ks[2], (L, RET_W), 0.01),
        'mla_q_norm_w': 1.0 + nrm(ks[3], (L, MLA_Q_RANK), 0.01),
        'mla_w_uq': nrm(ks[4], (L, MLA_Q_RANK, MLA_HEADS * (MLA_NOPE + MLA_ROPE)), MLA_Q_RANK ** -0.5),
        'mla_kv_norm_w': 1.0 + nrm(ks[5], (L, MLA_KV_RANK), 0.01),
        'mla_w_ukv': nrm(ks[6], (L, MLA_KV_RANK, MLA_HEADS * (MLA_NOPE + MLA_V)), MLA_KV_RANK ** -0.5) * jnp.asarray(ukv_scale),
        'mlstm_conv_w': nrm(ks[7], (L, MLSTM_CONV, 2 * MLSTM_W), MLSTM_CONV ** -0.5),
        'mlstm_conv_b': nrm(ks[8], (L, 2 * MLSTM_W), 0.01),
        'mlstm_b_i': nrm(ks[9], (L, MLSTM_HEADS), 0.1),
        'mlstm_b_f': jnp.linspace(3.0, 6.0, MLSTM_HEADS, dtype=jnp.float32)[None, :] + nrm(ks[10], (L, MLSTM_HEADS), 0.01),
        'mlstm_gn_w': 1.0 + nrm(ks[11], (L, MLSTM_W), 0.01),
        'w_out': nrm(ks[12], (L, MIX_W, D_MODEL), MIX_W ** -0.5 * DN_BETA),
        'ln1_w': 1.0 + nrm(ks[13], (L, D_MODEL), 0.01),
        'ln1_b': nrm(ks[14], (L, D_MODEL), 0.01),
        'ffn_w_gate': nrm(ks[15], (N_DENSE, D_MODEL, D_FF_2), D_MODEL ** -0.5),
        'ffn_w_up': nrm(ks[16], (N_DENSE, D_MODEL, D_FF_2), D_MODEL ** -0.5 * DN_BETA),
        'ffn_w_down': nrm(ks[17], (N_DENSE, D_FF_2, D_MODEL), D_FF_2 ** -0.5 * DN_BETA),
        'moe_router': nrm(ks[18], (N_MOE, D_MODEL, N_EXPERTS), D_MODEL ** -0.5),
        'moe_w_gate': nrm(ks[19], (N_MOE, N_EXPERTS, D_MODEL, D_FF_EXPERT), D_MODEL ** -0.5),
        'moe_w_up': nrm(ks[20], (N_MOE, N_EXPERTS, D_MODEL, D_FF_EXPERT), D_MODEL ** -0.5 * DN_BETA),
        'moe_w_down': nrm(ks[21], (N_MOE, N_EXPERTS, D_FF_EXPERT, D_MODEL), D_FF_EXPERT ** -0.5 * DN_BETA),
        'ln2_w': 1.0 + nrm(ks[22], (L, D_MODEL), 0.01),
        'ln2_b': nrm(ks[23], (L, D_MODEL), 0.01),
    }

def second_block(x, w_in, ret_gn_w, mla_q_norm_w, mla_w_uq, mla_kv_norm_w, mla_w_ukv, mlstm_conv_w, mlstm_conv_b, mlstm_b_i, mlstm_b_f, mlstm_gn_w, w_out, ln1_w, ln1_b, ffn_w_gate, ffn_w_up, ffn_w_down, moe_router, moe_w_gate, moe_w_up, moe_w_down, ln2_w, ln2_b):
    pos = jnp.arange(x.shape[1], dtype=jnp.float32)
    for l in range(DEPTH_2):
        mix = hybrid_mixer(x, pos, w_in[l], ret_gn_w[l], mla_q_norm_w[l], mla_w_uq[l], mla_kv_norm_w[l], mla_w_ukv[l], mlstm_conv_w[l], mlstm_conv_b[l], mlstm_b_i[l], mlstm_b_f[l], mlstm_gn_w[l], w_out[l])
        x = layer_norm(DN_ALPHA * x + mix, ln1_w[l], ln1_b[l])
        if l % 2 == 0:
            f = swiglu_2(x, ffn_w_gate[l // 2], ffn_w_up[l // 2], ffn_w_down[l // 2])
        else:
            f = moe_swiglu(x, moe_router[l // 2], moe_w_gate[l // 2], moe_w_up[l // 2], moe_w_down[l // 2])
        x = layer_norm(DN_ALPHA * x + f, ln2_w[l], ln2_b[l])
    return x


def setup_inputs(seed=0):
    out = dict(first_inputs(seed))
    for name, value in second_inputs(seed + 1).items():
        if name != "x":
            out[name + "_2"] = value
    return out


def reference(
    x, mix_norm_g, ffn_norm_g, final_norm_g, fox_w_in, fox_b_f, fox_w_out, s5_w_in, s5_a_re,
    s5_a_im, s5_log_dt, s5_b_re, s5_b_im, s5_c_re, s5_c_im, s5_d, s5_w_glu, pool_w, pool_b,
    pool_scale, ffn_w_gate_up, ffn_w_down, w_in_2, ret_gn_w_2, mla_q_norm_w_2, mla_w_uq_2,
    mla_kv_norm_w_2, mla_w_ukv_2, mlstm_conv_w_2, mlstm_conv_b_2, mlstm_b_i_2, mlstm_b_f_2,
    mlstm_gn_w_2, w_out_2, ln1_w_2, ln1_b_2, ffn_w_gate_2, ffn_w_up_2, ffn_w_down_2,
    moe_router_2, moe_w_gate_2, moe_w_up_2, moe_w_down_2, ln2_w_2, ln2_b_2,
):
    x = first_block(
        x, mix_norm_g, ffn_norm_g, final_norm_g, fox_w_in, fox_b_f, fox_w_out, s5_w_in, s5_a_re,
        s5_a_im, s5_log_dt, s5_b_re, s5_b_im, s5_c_re, s5_c_im, s5_d, s5_w_glu, pool_w, pool_b,
        pool_scale, ffn_w_gate_up, ffn_w_down,
    )
    return second_block(
        x, w_in_2, ret_gn_w_2, mla_q_norm_w_2, mla_w_uq_2, mla_kv_norm_w_2, mla_w_ukv_2,
        mlstm_conv_w_2, mlstm_conv_b_2, mlstm_b_i_2, mlstm_b_f_2, mlstm_gn_w_2, w_out_2,
        ln1_w_2, ln1_b_2, ffn_w_gate_2, ffn_w_up_2, ffn_w_down_2, moe_router_2, moe_w_gate_2,
        moe_w_up_2, moe_w_down_2, ln2_w_2, ln2_b_2,
    )


_drawn_inputs = setup_inputs


def setup_inputs(seed=0):
    import zlib

    import numpy as np

    out = dict(_drawn_inputs(seed))
    spreads = {}
    factors = {'s5_a_re': 62.792,
     'pool_b': 7.781,
     'ret_gn_w_2': 28.514,
     'mla_q_norm_w_2': 8.0,
     'mla_kv_norm_w_2': 8.0,
     'mlstm_conv_b_2': 8.0,
     'mlstm_b_i_2': 8.0,
     'mlstm_gn_w_2': 8.0,
     'ln1_w_2': 3.332,
     'ln1_b_2': 3.355,
     'ln2_w_2': 3.801,
     'ln2_b_2': 3.406}
    for name, (base, spread) in spreads.items():
        noise = np.random.default_rng([zlib.crc32(name.encode()), seed]).standard_normal(out[name].shape)
        drawn = base * np.exp(spread * noise) if base else spread * noise
        out[name] = jnp.asarray(drawn.astype(out[name].dtype))
    for name, factor in factors.items():
        out[name] = (out[name] * factor).astype(out[name].dtype)
    return out
```

```python
from contextlib import ExitStack

import numpy as np

import concourse.bass as bass
from concourse import mybir

P = 128
S = 256
TT = S // P
D = 1024
KD = D // P
DEPTH1 = 4
N_HEADS = 16
HD = 64
D_FF = 2816
EPS1 = 1e-6
EPS2 = 1e-5
G5, C5, P5 = 64, 16, 64
GPT = P // C5
WINDOWS = (2, 4, 8, 16)
N_EXP = 8
F_EXP = 3584
DEPTH2 = 2
DN_ALPHA = (2 * DEPTH2) ** 0.25
D_IN = 2472
MLA_H = 8
MLA_SCALE = float(96) ** -0.5
NEG = -1e30

RING = 4
SLOT = 6144
FC = 256
NSUB = FC // P
CAP = 128
PASSES = -(-S // CAP)

ALU = mybir.AluOpType
ACT = mybir.ActivationFunctionType
F32 = mybir.dt.float32
BF16 = mybir.dt.bfloat16
I32 = mybir.dt.int32
U32 = mybir.dt.uint32
AX = mybir.AxisListType

def constant_table():
    k, q = np.arange(P)[:, None], np.arange(P)[None, :]
    tok = np.arange(S, dtype=np.float64)
    cols = {}
    cols["ident"] = np.eye(P)
    diag = np.where(q <= k, 0.0, NEG)
    cols["fox_mask"] = np.concatenate([diag, np.zeros((P, P)), diag], 1)
    chunk = np.where(q < (k // 64 + 1) * 64, 0.0, NEG)
    cols["mla_mask"] = np.concatenate([chunk, np.zeros((P, P)), chunk], 1)
    up = np.where(q >= k, 0.0, NEG)
    cols["mlstm_mask"] = np.concatenate([up, np.zeros((P, P)), up], 1)
    lag = np.concatenate([q - k, q + P - k, q - k], 1).astype(np.float64)
    decay = []
    for h in range(4):
        lg = np.log(1.0 - 2.0 ** (-5.0 - h))
        decay.append(np.where(lag >= 0, np.exp(np.minimum(lag, 256) * lg * (lag >= 0)), 0.0) * HD ** -0.5)
    cols["ret_decay"] = np.concatenate(decay, 1)
    def rope(half):
        inv = 10000.0 ** (-np.arange(half, dtype=np.float32) / np.float32(half))
        ang = (np.arange(S, dtype=np.float32)[None, :] * inv[:, None].astype(np.float32)).astype(np.float32).astype(np.float64)
        return np.cos(ang), np.sin(ang)
    c, s = rope(32)
    cols["ret_cos"] = np.tile(c, (4, 1))
    cols["ret_sin"] = np.tile(s, (4, 1))
    c, s = rope(16)
    cols["mla_cos"] = np.concatenate([np.ones((64, S)), c, c, np.ones((32, S))], 0)
    cols["mla_sin"] = np.concatenate([np.zeros((64, S)), s, s, np.zeros((32, S))], 0)
    sw = np.zeros((P, P))
    for b in range(0, P, 64):
        for i in range(32):
            sw[b + 32 + i, b + i] = -1.0
            sw[b + i, b + 32 + i] = 1.0
    cols["ret_swap"] = sw
    sw = np.zeros((P, P))
    for i in range(16):
        sw[80 + i, 64 + i] = -1.0
        sw[64 + i, 80 + i] = 1.0
    cols["mla_swap"] = sw
    cols["before"] = (k < q) * 1.0
    cols["ones"] = np.ones((P, P))
    cols["tokens"] = np.tile(tok, (P, 1))
    for w in WINDOWS:
        cols[f"pool{w}"] = np.tile(1.0 / np.minimum(tok + 1, w), (P, 1))
    cols["half_sign"] = np.where(np.arange(P) < 64, -1.0, 1.0)[:, None]
    cols["row_group"] = (np.arange(P)[:, None] // C5 == np.arange(GPT)[None, :]) * 1.0
    cols["experts"] = np.tile(np.arange(N_EXP), (P, 1))
    at, out, n = {}, [], 0
    for name, v in cols.items():
        at[name] = (n, v.shape[1])
        out.append(v)
        n += v.shape[1]
    return at, np.ascontiguousarray(np.concatenate(out, 1).astype(np.float32))


VEC_ROWS = [("mix_norm_g", 32), ("ffn_norm_g", 32), ("s5_d", 8), ("mla_q_norm_w_2", 4), ("mla_kv_norm_w_2", 2),
            ("mlstm_conv_w_2", 32), ("mlstm_conv_b_2", 8), ("ret_gn_w_2", 4), ("mlstm_gn_w_2", 4)]
VEC_AT, _n = {}, 0
for _name, _k in VEC_ROWS:
    VEC_AT[_name] = _n
    _n += _k
VEC_TOTAL = _n
assert VEC_TOTAL <= P


class Tally:

    def __init__(self):
        self.count = {}
        self.loops = []

    def value(self, name):
        v = self.count.get(name, 0)
        for reg, adds, _, _ in self.loops:
            if adds.get(name, 0):
                v = reg * adds[name] + v
        return v

    def up(self, name, n=1):
        self.count[name] = self.count.get(name, 0) + n
        return self.value(name)

    def enter(self, reg, rounds, adds):
        self.loops.append((reg, adds, dict(self.count), rounds))

    def leave(self):
        reg, adds, before, rounds = self.loops.pop()
        for name, v in self.count.items():
            grown = v - before.get(name, 0)
            assert grown == adds.get(name, 0), (name, grown, adds.get(name, 0))
            self.count[name] = v + (rounds - 1) * grown
        for name in adds:
            assert name in self.count, name


_INS = ["x", "mix_norm_g", "ffn_norm_g", "final_norm_g", "fox_w_in", "fox_b_f", "fox_w_out", "s5_w_in", "s5_a_re",
        "s5_a_im", "s5_log_dt", "s5_b_re", "s5_b_im", "s5_c_re", "s5_c_im", "s5_d", "s5_w_glu", "pool_w", "pool_b",
        "pool_scale", "ffn_w_gate_up", "ffn_w_down", "w_in_2", "ret_gn_w_2", "mla_q_norm_w_2", "mla_w_uq_2",
        "mla_kv_norm_w_2", "mla_w_ukv_2", "mlstm_conv_w_2", "mlstm_conv_b_2", "mlstm_b_i_2", "mlstm_b_f_2",
        "mlstm_gn_w_2", "w_out_2", "ln1_w_2", "ln1_b_2", "ffn_w_gate_2", "ffn_w_up_2", "ffn_w_down_2",
        "moe_router_2", "moe_w_gate_2", "moe_w_up_2", "moe_w_down_2", "ln2_w_2", "ln2_b_2"]


def build(nc, inp, table, out):
    const_at, _ = constant_table()
    n_const = table.shape[1]
    ctx = ExitStack()
    with ctx:
        def sb(name, shape, dt=F32):
            return ctx.enter_context(nc.sbuf_tensor(name, shape, dt))

        def sem(name):
            return ctx.enter_context(nc.semaphore(name))

        ring = sb("ring", [P, RING, SLOT])
        x = sb("x_rows", [P, TT, D])
        xT = sb("xT", [P, KD, S])
        const = sb("const", [P, n_const])
        vec = sb("vec", [P, P])
        vec_rows = sb("vec_rows", [P, P])
        arena = sb("arena", [P, 17408])
        small = sb("small", [P, 256])
        marks = sb("marks", [1, 64])
        zeros = sb("zeros", [1, 512], BF16)
        heads_b = sb("heads_b", [P, 16])
        ps = ctx.enter_context(nc.psum_tensor("ps", [P, 8, 512], F32))

        def cst(name, p=P, lo=0, n=None):
            a, width = const_at[name]
            return const[0:p, a + lo:a + (width if n is None else lo + n)]

        ident = cst("ident")
        eps1, eps2, one = (small[:, 240 + i:241 + i] for i in range(3))

        def v_col(name, row, p0=0, p=P):
            c = VEC_AT[name] + row
            return vec[p0:p0 + p, c:c + 1]

        class Carve:

            def __init__(self):
                self.at = 0

            def __call__(self, *dims):
                n = int(np.prod(dims))
                a = arena[:, self.at:self.at + n]
                self.at += n
                assert self.at <= 17408, self.at
                if len(dims) == 1:
                    return a
                names = "abcd"[:len(dims)]
                kw = {c: d for c, d in zip(names[1:], dims[1:])}
                return a.rearrange(f"p ({' '.join(names)}) -> p {' '.join(names)}", **kw)

        cv = Carve()
        xn = cv(TT, D)
        prob = cv(2, 2, 3 * P)
        probT = cv(2, 2, 3 * P)
        qT, kT = cv(8, S), cv(8, S)
        v_rows = cv(TT, D)
        mixT = cv(KD, S)
        f_buf = cv(4, S)
        negC = cv(S)
        cv = Carve()
        cv(TT, D)
        silu = cv(2, NSUB * S)
        hid = cv(2, NSUB * S)

        cv = Carve()
        cv(TT, D)
        uT, gT = cv(8, S), cv(8, S)
        b_own, b_other = cv(G5, C5), cv(G5, C5)
        bb, bb_turn = cv(G5, C5), cv(G5, C5)
        c_T = cv(2, 8, P)
        c_in = cv(2, 8, P)
        c_pad_at = cv.at
        c_pad = cv(2, GPT, P)
        lam_in = cv(2, P)
        s5p = cv(12, G5)
        a_re, a_im, dt5, mag, phi_hi, phi_lo, k_re, k_im, t0, t1, t2, t3 = (s5p[:, i, :] for i in range(12))
        bT = arena[:, 6144:8192].rearrange("p (a k n) -> p a k n", a=2, k=8)
        b_pad = arena[:, 8192:8704].rearrange("p (a b n) -> p a b n", a=2, b=2)
        turns = arena[:, 8704:9216].rearrange("p (a n) -> p a n", a=2)
        turns_lo = arena[:, 1280:1792].rearrange("p (a n) -> p a n", a=2)
        whole = (arena[:, 9216:9472], arena[:, 1792:2048])
        w5 = arena[:, 9472:10240].rearrange("p (a n) -> p a n", a=3)
        rot = arena[:, 12288:13568].rearrange("p (a n) -> p a n", a=5)
        z_rot = arena[:, 0:1024].rearrange("p (a b n) -> p a b n", a=2, b=2)
        z_one = arena[:, 1024:1280]

        def zr(par, a):
            return z_rot[:, par, a, :]

        glu = arena[:, 2048:4096].rearrange("p (a n) -> p a n", a=4)
        cv = Carve()
        cv(TT, D)
        pool_s = cv(2, 2, S)
        row_tmp = cv(2, D)
        rowv = arena[:, 15360:17408].rearrange("p (a n) -> p a n", a=2)

        r_qk = arena[:, 0:1024].rearrange("p (a n) -> p a n", a=4)
        r_v = arena[:, 1024:1536].rearrange("p (a n) -> p a n", a=2)
        r_g = arena[:, 1536:2048].rearrange("p (a n) -> p a n", a=2)
        m_qk = arena[:, 5120:6144].rearrange("p (a n) -> p a n", a=4)
        m_v = arena[:, 6144:6664].rearrange("p (a h n) -> p a h n", a=2, h=4)
        m_o = arena[:, 6664:7176].rearrange("p (a n) -> p a n", a=2)
        gates = arena[:, 7176:9224].rearrange("p (a n) -> p a n", a=8)
        q_mla = arena[:, 5120:7168].rearrange("p (a n) -> p a n", a=8)
        k_mla = arena[:, 7168:9216].rearrange("p (a n) -> p a n", a=8)
        v_mla = arena[:, 9224:10248].rearrange("p (a n) -> p a n", a=2)
        cT = arena[:, 10248:11016].rearrange("p (a n) -> p a n", a=3)
        hn = arena[:, 13312:14336].rearrange("p (a n) -> p a n", a=16)
        tmp_a = arena[:, 14336:15360]

        def tmp_sq(i, n):
            return tmp_a[:, i * S:i * S + n]

        c_rows = arena[:, 0:768].rearrange("p (a n) -> p a n", a=2)
        kr_T = arena[:, 768:1024]
        vec_ml = small[:, 64:240]

        cv = Carve()
        acc = cv(TT, D)
        cv(2, NSUB * S), cv(2, NSUB * S)
        perm = cv(N_EXP, TT, CAP)
        perm_w = cv(N_EXP, TT, CAP)
        gate_T = cv(N_EXP, S)
        xe = cv(KD, CAP)
        y_e = cv(D)
        route = cv(10, TT, N_EXP)
        router = small[:, 128:192]
        route_idx = sb("route_idx", [P, TT, N_EXP], U32)
        overflow = sb("overflow", [P, 1], I32)
        M_CH = F_EXP // FC
        M_ROUNDS = (M_CH - 2) // RING
        M_LEFT = M_CH - 1 - M_ROUNDS * RING

        loaded = [sem(f"slot_loaded{i}") for i in range(RING)]
        released = [sem(f"slot_released{i}") for i in range(RING)]
        const_loaded = sem("const_loaded")
        x_loaded = sem("x_loaded")
        bias_loaded = sem("bias_loaded")
        vec_loaded = sem("vec_loaded")
        x_ready = sem("x_ready")
        full_act = sem("psum_full_for_act")
        full_dve = sem("psum_full_for_dve")
        drained_act = sem("act_drained_psum")
        drained_dve = sem("dve_drained_psum")
        act_to_dve = sem("act_result_for_dve")
        dve_to_act = sem("dve_result_for_act")
        dve_to_pe = sem("dve_result_for_pe")
        act_step = sem("act_step_done")
        dve_step = sem("dve_step_done")
        gate_full = sem("gate_full")
        up_full = sem("up_full")
        silu_ready = sem("silu_ready")
        hid_ready = sem("hidden_ready")
        act_to_pe = sem("act_result_for_pe")
        s5_loaded = sem("s5_parameters_loaded")
        bu_done = sem("s5_input_products_done")
        b_pad_ready = sem("s5_padded_b_ready")
        c_pad_ready = sem("s5_padded_c_ready")
        phase_ready = sem("s5_phase_ready")
        sin_ready = sem("s5_sines_ready")
        z_ready = sem("s5_rotated_states_ready")
        y_full = sem("s5_outputs_full")
        act_loop_step = sem("act_loop_step_done")
        dve_loop_step = sem("dve_loop_step_done")
        S5_LOADS = 16 * 11
        pool_step = sem("pool_step_done")
        turns_ready = sem("s5_turn_products_ready")
        rows_loaded = sem("row_vectors_loaded")
        rows_used = sem("row_vectors_used")
        overflow_ready = sem("overflow_flag_ready")
        router_loaded = sem("router_loaded")
        late_step = sem("dve_late_step_done")
        late_to_act = sem("last_variance_for_act")
        late_to_dve = sem("last_deviation_for_dve")
        out_stored = sem("out_stored")
        MAGIC = 1.5 * 2.0 ** 23
        PI = 3.1415925
        TWO_PI_HI, TWO_PI_LO = 6.28125, 2 * np.pi - 6.28125

        block = ctx.enter_context(nc.Block())

        gu1 = inp["ffn_w_gate_up"]
        FFNS = {("a", i): (gu1[i, :, 0:D_FF], gu1[i, :, D_FF:2 * D_FF], inp["ffn_w_down"][i]) for i in range(DEPTH1)}
        FFNS["b"] = (inp["ffn_w_gate_2"][0], inp["ffn_w_up_2"][0], inp["ffn_w_down_2"][0])
        N_CH = D_FF // FC
        ROUNDS = (N_CH - 2) // RING
        LEFT = N_CH - 1 - ROUNDS * RING

        def ring_adds(*extra):
            d = {f"loaded{i}": 48 for i in range(RING)}
            d.update({f"released{i}": 1 for i in range(RING)})
            d.update(dict(extra))
            return d

        @block.sync
        def _(sp):
            t = Tally()
            use = [0]
            sp.dma_start(x[:, :, :], inp["x"][0].rearrange("(t p) d -> p t d", p=P)).then_inc(x_loaded, 16)
            sp.dma_start(const[:, :], table).then_inc(const_loaded, 16)

            def slot_free():
                slot = use[0] % RING
                use[0] += 1
                if use[0] > RING:
                    sp.wait_ge(released[slot], t.up(f"released{slot}"))
                return slot

            def piece(w, c0, n, kt=KD):
                slot = slot_free()
                dst = ring[:, slot, 0:kt * n].rearrange("p (k n) -> p k n", n=n)
                src = w.rearrange("(k p) n -> p k n", p=P)[:, :, c0:c0 + n]
                cuts = [0, (kt + 2) // 3, (2 * kt + 2) // 3, kt] if kt > 2 else None
                if cuts:
                    for a, b in zip(cuts, cuts[1:]):
                        sp.dma_start(dst[:, a:b], src[:, a:b]).then_inc(loaded[slot], 16)
                else:
                    third = n // 4
                    for a, b in ((0, third), (third, 2 * third), (2 * third, n)):
                        sp.dma_start(dst[:, :, a:b], src[:, :, a:b]).then_inc(loaded[slot], 16)

            def chunk(gate, up, down, f0):
                slot = slot_free()
                for i, w in enumerate((gate, up)):
                    sp.dma_start(ring[:, slot, i * 2048:(i + 1) * 2048].rearrange("p (k n) -> p k n", n=FC),
                                 w.rearrange("(k p) n -> p k n", p=P)[:, :, bass.ds(f0, FC)]).then_inc(loaded[slot], 16)
                sp.dma_start(ring[:, slot, 4096:6144].rearrange("p (s n) -> p s n", n=D),
                             down[bass.ds(f0, FC), :].rearrange("(s p) n -> p s n", p=P)).then_inc(loaded[slot], 16)

            def ffn(key):
                gate, up, down = FFNS[key]
                chunk(gate, up, down, 0)
                with sp.Fori(0, ROUNDS) as i:
                    t.enter(i, ROUNDS, {f"released{j}": 1 for j in range(RING)})
                    for j in range(RING):
                        chunk(gate, up, down, i * (RING * FC) + (j + 1) * FC)
                    t.leave()
                for j in range(LEFT):
                    chunk(gate, up, down, (1 + ROUNDS * RING + j) * FC)

            def fox(j):
                w = inp["fox_w_in"][j]
                piece(w, 2560, 528)
                piece(w, 2048, 512)
                for c0 in (0, 512, 1024, 1536):
                    piece(w, c0, 512)
                for c0 in (0, 512):
                    piece(inp["fox_w_out"][j], c0, 512)

            def s5():
                piece(inp["s5_w_in"][0], 0, 512)
                piece(inp["s5_w_in"][0], 512, 512)
                for c0 in (0, D, 512, D + 512):
                    piece(inp["s5_w_glu"][0], c0, 512)

            def pool():
                piece(inp["pool_w"][0].rearrange("g c d -> (g c) d"), 0, S)

            fox(0)
            ffn(("a", 0))
            s5()
            ffn(("a", 1))
            pool()
            ffn(("a", 2))
            fox(1)
            ffn(("a", 3))
            def hybrid(l):
                w = inp["w_in_2"][l]
                for c0, n in ((0, 512), (512, 512), (1440, 512), (1952, 520), (1024, 416)):
                    piece(w, c0, n)
                piece(inp["mla_w_uq_2"][l], 0, 768, kt=2)
                piece(inp["mla_w_ukv_2"][l], 0, D, kt=1)
                for c0 in (0, 512):
                    piece(inp["w_out_2"][l], c0, 512)

            hybrid(0)
            ffn("b")
            hybrid(1)
            def moe_pass():
                for e in range(N_EXP):
                    gate, up, down = (inp[k][0, e] for k in ("moe_w_gate_2", "moe_w_up_2", "moe_w_down_2"))
                    chunk(gate, up, down, 0)
                    with sp.Fori(0, M_ROUNDS) as i:
                        t.enter(i, M_ROUNDS, {f"released{j}": 1 for j in range(RING)})
                        for j in range(RING):
                            chunk(gate, up, down, i * (RING * FC) + (j + 1) * FC)
                        t.leave()
                    for j in range(M_LEFT):
                        chunk(gate, up, down, (1 + M_ROUNDS * RING + j) * FC)

            moe_pass()
            sp.wait_ge(overflow_ready, 1)
            more = sp.value_load(overflow[0:1, 0:1], min_val=0, max_val=1)
            with sp.If(more > 0):
                for _ in range(1, PASSES):
                    moe_pass()
            sp.wait_ge(out_stored, 16)

        @block.scalar
        def _(act):
            t = Tally()
            for name, n in VEC_ROWS:
                src = inp[name]
                if len(src.shape) == 2:
                    src = src.rearrange("l (k p) -> (l k) p", p=P)
                else:
                    src = src.rearrange("l t (k p) -> (l t k) p", p=P)
                a = VEC_AT[name]
                act.dma_start(vec_rows[a:a + n, :], src).then_inc(vec_loaded, 16)
            for j in range(2):
                act.dma_start(heads_b[0:16, j:j + 1], inp["fox_b_f"][j].rearrange("(h o) -> h o", o=1)).then_inc(bias_loaded, 16)
                act.dma_start(heads_b[0:4, 2 + j:3 + j], inp["mlstm_b_i_2"][j].rearrange("(h o) -> h o", o=1)).then_inc(bias_loaded, 16)
                act.dma_start(heads_b[0:4, 4 + j:5 + j], inp["mlstm_b_f_2"][j].rearrange("(h o) -> h o", o=1)).then_inc(bias_loaded, 16)

            def then(ins):
                ins.then_inc(act_step, 1)
                act.wait_ge(act_step, t.up("act_step"))

            def drain(ins):
                ins.then_inc(drained_act, 1)
                return t.up("drained_act")

            def full():
                act.wait_ge(full_act, t.up("full_act"))

            def rms_xT(ver, g, for_dve=False):
                act.wait_ge(x_ready, ver)
                for i in range(TT):
                    ins = act.activation(xn[:, i, :], x[:, i, :], ACT.Square, accum_out=small[:, i:i + 1])
                then(ins)
                act.activation(small[:, 4:6], small[:, 0:2], ACT.Sqrt, scale=1.0 / D, bias=eps1).then_inc(act_to_dve, 1)
                xT_banks(g, for_dve)

            def xT_banks(g, for_dve=False):
                for j in (0, 2):
                    full()
                    for kk in range(2):
                        k = 2 * j + kk
                        ins = act.activation(xT[:, k, :], ps[:, j, kk * S:(kk + 1) * S], ACT.Copy,
                                             scale=(1.0 if g is None else vec[:, g + k:g + k + 1]))
                    if for_dve and j == 2:
                        ins.then_inc(act_to_dve, 1)
                    else:
                        drain(ins)

            def ffn(n_tok=S):
                def one():
                    act.wait_ge(gate_full, t.up("gate_full"))
                    par = (t.count["gate_full"] - 1) % 2
                    if t.count["gate_full"] > 1:
                        act.wait_ge(hid_ready, t.value("gate_full") - 1)
                    act.activation(silu[:, par, :], ps[:, 2 * par, :], ACT.Silu).then_inc(silu_ready, 1)
                one()
                with act.Fori(0, ROUNDS) as i:
                    t.enter(i, ROUNDS, {"gate_full": RING})
                    for _ in range(RING):
                        one()
                    t.leave()
                for _ in range(LEFT):
                    one()

            def fox(j):
                full()
                act.wait_ge(bias_loaded, 96)
                ins = act.activation(f_buf[0:16, 0, :], ps[0:16, 0, 0:S], ACT.Identity, bias=heads_b[0:16, j:j + 1])
                act.wait_ge(drained_act, drain(ins))
                then(act.activation(f_buf[0:16, 1, :], f_buf[0:16, 0, :], ACT.Abs))
                then(act.activation(f_buf[0:16, 1, :], f_buf[0:16, 1, :], ACT.Exp, scale=-1.0))
                act.activation(f_buf[0:16, 1, :], f_buf[0:16, 1, :], ACT.Ln, bias=one[0:16]).then_inc(act_to_dve, 1)
                for i in range(4):
                    full()
                    drain(act.activation(qT[:, 2 * i:2 * i + 2, :],
                                         ps[:, (5 + i) % 8, :].rearrange("p (a b) -> p a b", b=S), ACT.Copy,
                                         scale=HD ** -0.5))
                attend(8)

            def attend(pairs):
                for i in range(pairs + 1):
                    if i < pairs:
                        act.wait_ge(dve_to_act, t.up("dve_to_act"))
                        for r in range(2):
                            for q, (a, b) in enumerate(((0, P), (P, 3 * P))):
                                c = 16 + 8 * (i % 2) + 2 * q + r
                                ins = act.activation(prob[:, i % 2, r, a:b], prob[:, i % 2, r, a:b], ACT.Exp,
                                                     bias=small[:, c:c + 1], accum_out=small[:, c + 4:c + 5])
                        ins.then_inc(act_to_dve, 1)
                    if i >= 1:
                        full()
                        drain(act.activation(probT[:, (i - 1) % 2, :, :], ps[:, 4:6, 0:3 * P], ACT.Copy))

            def then_in(ins, T, k):
                ins.then_inc(act_loop_step, 1)
                act.wait_ge(act_loop_step, T * (2 * GPT) + k)

            def s5():
                act.wait_ge(s5_loaded, S5_LOADS)
                act.activation(dt5, dt5, ACT.Exp).then_inc(act_to_dve, 1)
                act.wait_ge(dve_to_act, t.up("dve_to_act"))
                act.activation(mag, t0, ACT.Exp)
                act.activation(t2, t1, ACT.Sin, scale=0.5)
                act.activation(t3, t1, ACT.Sin).then_inc(act_to_dve, 1)
                rms_xT(3, VEC_AT["mix_norm_g"] + KD)
                for i in range(4):
                    full()
                    drain(act.activation(uT[:, 2 * i:2 * i + 2, :], ps[:, 4 + i, :].rearrange("p (a b) -> p a b", b=S),
                                         ACT.Copy))
                act.wait_ge(dve_to_act, t.up("dve_to_act"))

                def turn_products(g):
                    act.activation(turns[:, g % 2, :], cst("tokens"), ACT.Copy, scale=phi_hi[:, g:g + 1])
                    act.activation(turns_lo[:, g % 2, :], cst("tokens"), ACT.Copy, scale=phi_lo[:, g:g + 1])\
                       .then_inc(turns_ready, 1)
                turn_products(0)
                turn_products(1)
                for T in range(8):
                    for j in range(GPT):
                        par = j % 2
                        act.wait_ge(bu_done, T * GPT + j + 1)
                        for a in range(2):
                            ins = act.activation(b_pad[:, a, par, :], bT[:, a, bass.ds(T, 1), :].squeeze(1), ACT.Copy,
                                                 scale=cst("row_group")[:, j:j + 1])
                        ins.then_inc(b_pad_ready, 1)
                        act.wait_ge(phase_ready, T * GPT + (j + 1))
                        act.wait_ge(z_ready, T * GPT + (j + 1))
                        act.activation(rot[:, par, :], turns[:, par, :], ACT.Sin, scale=2 * PI)
                        act.wait_ge(sin_ready, T * GPT + (j + 2))
                        then_in(act.activation(rot[:, 4, :], turns[:, par, :], ACT.Sin, scale=PI), T, 2 * j + 1)
                        then_in(act.activation(rot[:, 4, :], rot[:, 4, :], ACT.Square), T, 2 * j + 2)
                        act.activation(rot[:, 2 + par, :], rot[:, 4, :], ACT.Identity, scale=-2.0, bias=one)\
                           .then_inc(sin_ready, 1)
                        if T * GPT + j + 2 < G5:
                            turn_products(T * GPT + j + 2)
                act.wait_ge(dve_to_act, t.up("dve_to_act"))
                act.activation(gT[:, :, :], gT[:, :, :], ACT.Gelu_apprx_tanh).then_inc(act_to_pe, 1)
                for c in range(2):
                    for i in range(TT):
                        full()
                        act.activation(glu[:, 2 * c + i, :], ps[:, 4 * c + 2 + i, :], ACT.Sigmoid).then_inc(act_to_dve, 1)
            rms_xT(1, VEC_AT["mix_norm_g"])
            fox(0)
            rms_xT(2, VEC_AT["ffn_norm_g"])
            ffn()
            s5()
            rms_xT(4, VEC_AT["ffn_norm_g"] + KD)
            ffn()
            rms_xT(5, VEC_AT["mix_norm_g"] + 2 * KD, for_dve=True)
            rms_xT(6, VEC_AT["ffn_norm_g"] + 2 * KD)
            ffn()
            rms_xT(7, VEC_AT["mix_norm_g"] + 3 * KD)
            fox(1)
            rms_xT(8, VEC_AT["ffn_norm_g"] + 3 * KD)
            ffn()
            def rows_rms(ver):
                act.wait_ge(x_ready, ver)
                for i in range(TT):
                    ins = act.activation(xn[:, i, :], x[:, i, :], ACT.Square, accum_out=small[:, i:i + 1])
                then(ins)
                act.activation(small[:, 4:6], small[:, 0:2], ACT.Sqrt, scale=1.0 / D, bias=eps1).then_inc(act_to_dve, 1)

            def ln():
                act.wait_ge(dve_to_act, t.up("dve_to_act"))
                act.activation(small[:, 4:6], small[:, 44:46], ACT.Sqrt, bias=eps2).then_inc(act_to_dve, 1)

            def hybrid(l):
                xT_banks(None)
                full()
                drain(act.activation(r_qk, ps[:, 4:6, :].rearrange("p b (a n) -> p (b a) n", a=2), ACT.Copy))
                for i in range(TT):
                    full()
                    act.activation(r_v[:, i, :], ps[:, 6 + i, 0:S], ACT.Copy)
                    drain(act.activation(r_g[:, i, :], ps[:, 6 + i, S:2 * S], ACT.Silu))
                for i in range(TT):
                    full()
                    act.activation(m_v[:, i, :, 0:HD], ps[:, 4 + i, 0:S].rearrange("p (h n) -> p h n", n=HD), ACT.Copy)
                    drain(act.activation(m_o[:, i, :], ps[:, 4 + i, S:2 * S], ACT.Sigmoid))
                full()
                act.activation(gates[0:4, 0, :], ps[0:4, 6, 0:S], ACT.Identity, bias=heads_b[0:4, 2 + l:3 + l])
                ins = act.activation(gates[0:4, 1, :], ps[0:4, 6, S:2 * S], ACT.Identity, bias=heads_b[0:4, 4 + l:5 + l])
                act.wait_ge(drained_act, drain(ins))
                then(act.activation(gates[0:4, 2, :], gates[0:4, 1, :], ACT.Abs))
                then(act.activation(gates[0:4, 2, :], gates[0:4, 2, :], ACT.Exp, scale=-1.0))
                act.activation(gates[0:4, 2, :], gates[0:4, 2, :], ACT.Ln, bias=one[0:4]).then_inc(act_to_dve, 1)
                act.wait_ge(dve_to_act, t.up("dve_to_act"))
                act.activation(m_qk, m_qk, ACT.Silu).then_inc(act_to_pe, 1)
                full()
                drain(act.activation(vec_ml[:, 0:8], ps[:, 5, 0:8], ACT.Exp))
                for p in range(2):
                    act.wait_ge(dve_to_act, t.up("dve_to_act"))
                    act.activation(probT[:, p], probT[:, p], ACT.Exp).then_inc(act_to_dve, 1)
                for i in range(TT):
                    full()
                    ins = act.activation(c_rows[:, i, :], ps[:, i, 0:384], ACT.Copy)
                    act.wait_ge(drained_act, drain(ins))
                full()
                drain(act.activation(kr_T[64:96, :], ps[64:96, 2, 0:S], ACT.Copy))
                for i in range(TT):
                    act.activation(tmp_sq(i, S), c_rows[:, i, 0:S], ACT.Square, accum_out=vec_ml[:, 8 + i:9 + i])
                    ins = act.activation(tmp_sq(2 + i, P), c_rows[:, i, S:384], ACT.Square, accum_out=vec_ml[:, 10 + i:11 + i])
                then(ins)
                act.activation(vec_ml[:, 12:14], vec_ml[:, 8:10], ACT.Sqrt, scale=1.0 / 256, bias=eps2)
                act.activation(vec_ml[:, 14:16], vec_ml[:, 10:12], ACT.Sqrt, scale=1.0 / 128, bias=eps2).then_inc(act_to_dve, 1)
                full()
                for c in range(3):
                    src = ps[:, 6 + c // 2, (c % 2) * S:(c % 2 + 1) * S]
                    wv = v_col("mla_q_norm_w_2", 2 * l + c) if c < 2 else v_col("mla_kv_norm_w_2", l)
                    ins = act.activation(cT[:, c, :], src, ACT.Copy, scale=wv)
                drain(ins)
                act.wait_ge(dve_to_act, t.up("dve_to_act"))
                act.activation(vec_ml[:, 32:48], vec_ml[:, 32:48], ACT.Sqrt, scale=1.0 / HD, bias=eps2).then_inc(act_to_dve, 1)
                for n, b in enumerate((0, 1, 2, 4)):
                    full()
                    drain(act.activation(q_mla[0:96, 2 * n:2 * n + 2, :], ps[0:96, b, :].rearrange("p (a n) -> p a n", a=2),
                                         ACT.Copy, scale=MLA_SCALE))
                full()
                for c in range(4):
                    name, dst = ("ret_gn_w_2", c) if c < 2 else ("mlstm_gn_w_2", 4 + c)
                    ins = act.activation(mixT[:, dst, :], ps[:, 5 + c // 2, (c % 2) * S:(c % 2 + 1) * S], ACT.Copy,
                                         scale=v_col(name, 2 * l + c % 2))
                drain(ins)
                for n in range(4):
                    full()
                    drain(act.activation(k_mla[0:HD, 2 * n:2 * n + 2, :],
                                         ps[0:HD, (0, 1, 2, 4)[n], :].rearrange("p (a n) -> p a n", a=2), ACT.Copy))
                attend(4)

            rows_rms(9)
            act.wait_ge(x_ready, 10)
            hybrid(0)
            ln()
            xT_banks(None)
            ffn()
            ln()
            hybrid(1)
            ln()
            def moe_pass():
                full()
                drain(act.activation(xe.rearrange("p (b a) n -> p b (a n)", b=2), ps[:, 6:8, 0:4 * CAP], ACT.Copy))
                for e in range(N_EXP):
                    def one():
                        act.wait_ge(gate_full, t.up("gate_full"))
                        par = (t.count["gate_full"] - 1) % 2
                        act.wait_ge(hid_ready, t.value("gate_full") - 1)
                        act.activation(silu[:, par, 0:NSUB * CAP], ps[:, par, 0:NSUB * CAP], ACT.Silu).then_inc(silu_ready, 1)
                    one()
                    with act.Fori(0, M_ROUNDS) as i:
                        t.enter(i, M_ROUNDS, {"gate_full": RING})
                        for _ in range(RING):
                            one()
                        t.leave()
                    for _ in range(M_LEFT):
                        one()
                    full()
                    drain(act.activation(y_e[0:CAP, :].rearrange("p (b n) -> p b n", b=2), ps[0:CAP, 4:6, :], ACT.Copy))
                    if e < N_EXP - 1:
                        full()
                        drain(act.activation(xe.rearrange("p (b a) n -> p b (a n)", b=2), ps[:, 6:8, 0:4 * CAP], ACT.Copy))

            xT_banks(None)
            act.wait_ge(dve_to_act, t.up("dve_to_act"))
            act.activation(route[:, 9, :, 0:1], route[:, 9, :, 0:1], ACT.Exp).then_inc(act_to_dve, 1)
            moe_pass()
            act.wait_ge(overflow_ready, 1)
            more = act.value_load(overflow[0:1, 0:1], min_val=0, max_val=1)
            with act.If(more > 0):
                for _ in range(1, PASSES):
                    moe_pass()
            act.wait_ge(late_to_act, 1)
            act.activation(small[:, 4:6], small[:, 44:46], ACT.Sqrt, bias=eps2).then_inc(late_to_dve, 1)
            act.wait_ge(x_ready, 14)
            act.dma_start(out[0].rearrange("(t p) d -> p t d", p=P), x[:, :, :]).then_inc(out_stored, 16)

        @block.gpsimd
        def _(pool):
            pool.wait_ge(x_ready, 2)
            n = 0
            br, bi = (inp[k][0].rearrange("g p c -> p g c") for k in ("s5_b_re", "s5_b_im"))
            cr, ci = (inp[k][0].rearrange("(k g) c p -> (g c) k p", g=GPT) for k in ("s5_c_re", "s5_c_im"))
            loads = [(b_own[0:64], br), (b_own[64:P], bi), (b_other[0:64], bi), (b_other[64:P], br),
                     (c_in[:, 0, :, 0:64], cr), (c_in[:, 0, :, 64:P], ci)]
            for half in (slice(0, 64), slice(64, P)):
                loads += [(lam_in[0:G5, 0, half], inp["s5_a_re"][0]), (lam_in[0:G5, 1, half], inp["s5_a_im"][0])]
            loads += [(dt5, inp["s5_log_dt"].broadcast_to([P, G5]))]
            for dst, src in loads:
                pool.dma_start(dst, src, allow_slow_non_contiguous=True).then_inc(s5_loaded, 16)
                n += 16
            assert n == S5_LOADS, n
            for T in range(8):
                for j in range(GPT):
                    par = j % 2
                    pool.wait_ge(turns_ready, T * GPT + (j + 1))

                    def step(ins, k):
                        ins.then_inc(pool_step, 1)
                        pool.wait_ge(pool_step, T * (4 * GPT) + 4 * j + k)
                    o = turns[:, par, :]
                    step(pool.tensor_scalar(whole[par], o, MAGIC, MAGIC, ALU.add, ALU.subtract), 1)
                    step(pool.tensor_tensor(o, o, whole[par], ALU.subtract), 2)
                    step(pool.tensor_tensor(o, o, turns_lo[:, par, :], ALU.add), 3)
                    step(pool.tensor_scalar(whole[par], o, MAGIC, MAGIC, ALU.add, ALU.subtract), 4)
                    pool.tensor_tensor(o, o, whole[par], ALU.subtract).then_inc(phase_ready, 1)
            pool.dma_start(router.rearrange("p (k e) -> p k e", e=N_EXP),
                           inp["moe_router_2"][0].rearrange("(k p) e -> p k e", p=P)).then_inc(router_loaded, 16)
            def row(k, src):
                pool.dma_start(rowv[:, k, :], src.broadcast_to([P, D])).then_inc(rows_loaded, 16)
            pool.wait_ge(x_ready, 4)
            row(0, inp["pool_b"])
            row(1, inp["pool_scale"])
            pool.wait_ge(x_ready, 6)
            row(0, inp["final_norm_g"].rearrange("(o d) -> o d", o=1))
            for n, (wn, bn, l) in enumerate((("ln1_w_2", "ln1_b_2", 0), ("ln2_w_2", "ln2_b_2", 0),
                                             ("ln1_w_2", "ln1_b_2", 1), ("ln2_w_2", "ln2_b_2", 1))):
                pool.wait_ge(x_ready, 10 + n)
                row(0, inp[wn][l:l + 1, :])
                row(1, inp[bn][l:l + 1, :])

        @block.tensor
        def _(pe):
            t = Tally()
            use = [0]
            holder = {}

            def take():
                slot = use[0] % RING
                use[0] += 1
                pe.wait_ge(loaded[slot], t.up(f"loaded{slot}", 48))
                return slot

            def claim(*banks):
                for b in banks:
                    if b in holder:
                        pe.wait_ge(*holder.pop(b))

            def to_act(ins, *banks):
                ins.then_inc(full_act, 1)
                tk = (drained_act, t.up("drained_act"))
                for b in banks:
                    holder[b] = tk
                return tk

            def to_dve(ins, *banks):
                ins.then_inc(full_dve, 1)
                tk = (drained_dve, t.up("drained_dve"))
                for b in banks:
                    holder[b] = tk
                return tk

            done_with = []

            def release(slot):
                done_with.append(slot)

            def carry(ins):
                if done_with:
                    ins.then_inc(released[done_with.pop()], 1)
                return ins

            def to_x(ins, *banks):
                ins.then_inc(full_dve, 1)
                tk = (x_ready, t.up("x_ready"))
                for b in banks:
                    holder[b] = tk

            def feats(o, w, c0, m, rhs, kt=KD):
                for k in range(kt):
                    ins = pe.matmul(o, lhsT=w[:, k, c0:c0 + m], rhs=rhs[:, k, :], start=(k == 0), stop=(k == kt - 1))
                    if k == 0:
                        carry(ins)
                return ins

            def rows(o, lhs, i, w, c0, n, kt=KD, k0=0):
                for k in range(kt):
                    ins = pe.matmul(o, lhsT=lhs[:, k0 + k, i * P:(i + 1) * P], rhs=w[:, k, c0:c0 + n],
                                    start=(k == 0), stop=(k == kt - 1))
                    if k == 0:
                        carry(ins)
                return ins

            def wslot(n, kt=KD):
                slot = take()
                return slot, ring[:, slot, 0:kt * n].rearrange("p (k n) -> p k n", n=n)

            def turn(src, for_dve=False):
                tks = []
                for j in range(4):
                    claim(j)
                    for kk in range(2):
                        for i in range(TT):
                            k = 2 * j + kk
                            ins = pe.transpose(ps[:, j, (kk * TT + i) * P:(kk * TT + i + 1) * P],
                                               src[:, i, k * P:(k + 1) * P], ident)
                            if j == kk == i == 0:
                                carry(ins)
                    if for_dve and j == 2:
                        ins.then_inc(full_act, 1)
                        tks.append(None)
                    else:
                        tks.append((to_act if j % 2 == 0 else to_dve)(ins, j))
                return tks

            def xT_ready(tks):
                for tk in tks[2:]:
                    pe.wait_ge(*tk)

            def rms_xT(for_dve=False):
                pe.wait_ge(dve_to_pe, t.up("dve_to_pe"))
                tks = turn(xn, for_dve)
                if not for_dve:
                    xT_ready(tks)

            def ffn(plain=True):
                claim(*range(8))
                for b in range(4, 8):
                    pe.matmul(ps[:, b, :], lhsT=zeros[0:1, 0:P], rhs=zeros[0:1, :], start=True, stop=False,
                              skip_group_check=True)
                slots = []

                def gate_up():
                    slot = take()
                    slots.append(slot)
                    par = t.count.get("chunk", 0) % 2
                    t.up("chunk")
                    for half, full in ((0, gate_full), (1, up_full)):
                        w = ring[:, slot, half * 2048:(half + 1) * 2048].rearrange("p (k n) -> p k n", n=FC)
                        for s in range(NSUB):
                            ins = feats(ps[:, 2 * par + half, s * S:(s + 1) * S], w, s * P, P, xT)
                        ins.then_inc(full, 1)

                def down(last=False):
                    slot = slots[-1] if last else slots[-2]
                    par = (t.count["hid_ready"] - 1) % 2
                    pe.wait_ge(hid_ready, t.up("hid_ready"))
                    w = ring[:, slot, 4096:6144].rearrange("p (s n) -> p s n", n=D)
                    for s in range(NSUB):
                        for i in range(TT):
                            for c in range(2):
                                ins = pe.matmul(ps[:, 4 + 2 * i + c, :],
                                                lhsT=hid[:, par, s * S + i * P:s * S + (i + 1) * P],
                                                rhs=w[:, s, c * 512:(c + 1) * 512], start=False,
                                                stop=last and s == NSUB - 1, skip_group_check=True)
                    ins.then_inc(released[slot], 1)

                gate_up()
                with pe.Fori(0, ROUNDS) as i:
                    adds = {f"loaded{j}": 48 for j in range(RING)}
                    adds.update(chunk=RING, hid_ready=RING)
                    t.enter(i, ROUNDS, adds)
                    for _ in range(RING):
                        gate_up()
                        down()
                    t.leave()
                for _ in range(LEFT):
                    gate_up()
                    down()
                down(last=True)
                for b in range(4, 8):
                    ins = pe.matmul(ps[:, b, :], lhsT=zeros[0:1, 0:P], rhs=zeros[0:1, :], start=False, stop=True,
                                    skip_group_check=True)
                (to_x if plain else to_dve)(ins, 4, 5, 6, 7)

            def mix_out(plain=True):
                for c in range(2):
                    slot, w = wslot(512)
                    for i in range(TT):
                        b = 2 * c + i
                        claim(b)
                        ins = rows(ps[:, b, :], mixT, i, w, 0, 512)
                        if c == i == 1 and plain:
                            to_x(ins, b)
                        else:
                            to_dve(ins, b)
                    release(slot)

            def fox(j):
                slot, w = wslot(528)
                claim(0)
                to_act(feats(ps[0:16, 0, 0:S], w, 512, 16, xT), 0)
                for i in range(TT):
                    claim(1 + i)
                    ins = rows(ps[:, 1 + i, :], xT, i, w, 0, 512)
                    to_dve(ins, 1 + i)
                release(slot)
                slot, w = wslot(512)
                for i in range(TT):
                    claim(3 + i)
                    ins = rows(ps[:, 3 + i, :], xT, i, w, 0, 512)
                    to_dve(ins, 3 + i)
                release(slot)
                b = 5
                for to in (to_act, to_dve):
                    for c in range(2):
                        slot, w = wslot(512)
                        for m in range(4):
                            if m % 2 == 0:
                                claim(b % 8)
                            ins = feats(ps[:, b % 8, (m % 2) * S:(m % 2 + 1) * S], w, m * P, P, xT)
                            if m % 2 == 1:
                                tk = to(ins, b % 8)
                                b += 1
                        release(slot)
                        if to is to_act:
                            q_tk = tk
                pe.wait_ge(*q_tk)
                pe.wait_ge(*tk)
                pe.wait_ge(dve_to_pe, t.up("dve_to_pe"))

                def score(i, r, o, q0, n):
                    p0 = HD * r
                    h = 2 * i + r
                    pe.matmul(o, lhsT=qT[p0:p0 + HD, i, q0:q0 + P], rhs=kT[p0:p0 + HD, i, 0:n], start=True, stop=False)
                    return pe.matmul(o, lhsT=ident[p0:p0 + HD, p0 + h:p0 + h + 1].to_broadcast([HD, P]),
                                     rhs=negC[p0:p0 + HD, 0:n], start=False, stop=True)

                attend(8, score, lambda i, r, kt: v_rows[:, kt, (2 * i + r) * HD:(2 * i + r + 1) * HD])
                mix_out()

            def s5():
                pe.wait_ge(s5_loaded, S5_LOADS)
                claim(0, 1, 2, 3, 4)
                for a in range(2):
                    ins = carry(pe.transpose(ps[:, 0, a * G5:(a + 1) * G5], lam_in[0:G5, a, :], ident[0:G5, 0:G5]))
                to_dve(ins, 0)
                pe.wait_ge(dve_to_pe, t.up("dve_to_pe"))
                for a in range(2):
                    for k in range(8):
                        b = 1 + 2 * a + k // 4
                        ins = pe.transpose(ps[:, b, (k % 4) * P:(k % 4 + 1) * P], c_in[:, a, k, :], ident)
                to_dve(ins, 1, 2, 3, 4)
                pe.wait_ge(dve_to_pe, t.up("dve_to_pe"))
                claim(5, 6, 7, 0)
                for a, src in enumerate((bb, bb_turn)):
                    for k in range(8):
                        b = (5 + 2 * a + k // 4) % 8
                        ins = pe.transpose(ps[:, b, (k % 4) * P:(k % 4 + 1) * P],
                                           src[:, k * GPT:(k + 1) * GPT, :].rearrange("p g c -> p (g c)"), ident)
                to_dve(ins, 5, 6, 7, 0)
                rms_xT()
                for c in range(2):
                    slot, w = wslot(512)
                    for m in range(4):
                        b = 4 + 2 * c + m // 2
                        if m % 2 == 0:
                            claim(b)
                        ins = feats(ps[:, b, (m % 2) * S:(m % 2 + 1) * S], w, m * P, P, xT)
                        if m % 2 == 1:
                            tk = to_act(ins, b)
                    release(slot)
                pe.wait_ge(*tk)
                claim(*range(8))

                def y_part(T, j):
                    par = j % 2
                    pe.wait_ge(z_ready, T * GPT + (j + 3))
                    for a in range(2):
                        ins = pe.matmul(ps[:, 6, 0:S], lhsT=c_pad[:, a, j, :], rhs=zr(par, a), start=(a == 0 and j == 0),
                                        stop=(a == 1 and j == GPT - 1))
                    return ins

                with pe.Fori(0, 8) as T:
                    for j in range(GPT):
                        par = j % 2
                        pe.wait_ge(b_pad_ready, T * GPT + (j + 1))
                        for a in range(2):
                            ins = pe.matmul(ps[:, par, a * S:(a + 1) * S], lhsT=b_pad[:, a, par, :],
                                            rhs=uT[:, bass.ds(T, 1), :].squeeze(1), start=True, stop=True)
                        ins.then_inc(bu_done, 1)
                        if j == 1:
                            pe.wait_ge(c_pad_ready, T + 1)
                        if j >= 1:
                            y_part(T, j - 1)
                    y_part(T, GPT - 1).then_inc(y_full, 1)
                pe.wait_ge(act_to_pe, t.up("act_to_pe"))
                for c in range(2):
                    for half in range(2):
                        slot, w = wslot(512)
                        for i in range(TT):
                            b = 4 * c + 2 * half + i
                            claim(b)
                            ins = rows(ps[:, b, :], gT, i, w, 0, 512)
                            if half:
                                ins.then_inc(full_act, 1)
                                holder[b] = (x_ready, t.value("x_ready") + 1)
                            else:
                                to_dve(ins, b)
                        release(slot)
                t.up("x_ready")

            def pool():
                pe.wait_ge(dve_to_pe, t.up("dve_to_pe"))
                slot, w = wslot(S)
                for i in range(TT):
                    for c in range(2):
                        claim(2 * i + c)
                        for g in range(2):
                            gi = 2 * c + g
                            ins = rows(ps[:, 2 * i + c, g * S:(g + 1) * S], mixT, i, w[:, 2 * gi:2 * gi + 2, :], 0, S,
                                       kt=2, k0=2 * gi)
                        to_dve(ins, 2 * i + c)
                release(slot)
                t.up("x_ready")

            def attend(pairs, score, v_of):
                pt = {}
                for i in range(pairs + 2):
                    if i < pairs:
                        b0 = 2 * (i % 2)
                        claim(b0, b0 + 1)
                        for r in range(2):
                            score(i, r, ps[:, b0 + r, 0:P], 0, P)
                            ins = score(i, r, ps[:, b0 + r, P:3 * P], P, S)
                        to_dve(ins, b0, b0 + 1)
                    if 1 <= i <= pairs:
                        pe.wait_ge(dve_to_pe, t.up("dve_to_pe"))
                        claim(4, 5)
                        for r in range(2):
                            for c in range(3):
                                ins = pe.transpose(ps[:, 4 + r, c * P:(c + 1) * P],
                                                   prob[:, (i - 1) % 2, r, c * P:(c + 1) * P], ident)
                        pt[i - 1] = to_act(ins, 4, 5)
                    if i >= 2:
                        h = i - 2
                        pe.wait_ge(*pt[h])
                        b = 6 + h % 2
                        claim(b)
                        for r in range(2):
                            o = ps[HD * r:HD * r + HD, b, :]
                            pe.matmul(o[:, 0:S], lhsT=v_of(h, r, 0), rhs=probT[:, h % 2, r, 0:S], start=True, stop=False,
                                      skip_group_check=True)
                            ins = pe.matmul(o[:, P:S], lhsT=v_of(h, r, 1), rhs=probT[:, h % 2, r, S:3 * P], start=False,
                                            stop=True, skip_group_check=True)
                        tk = to_dve(ins, b)
                pe.wait_ge(*tk)

            t.up("x_ready")
            t.up("hid_ready")
            pe.wait_ge(const_loaded, 16)
            pe.wait_ge(vec_loaded, 16 * len(VEC_ROWS))
            to_dve(pe.transpose(ps[:, 7, 0:VEC_TOTAL], vec_rows[0:VEC_TOTAL, :], ident[0:VEC_TOTAL, 0:VEC_TOTAL]), 7)
            rms_xT()
            fox(0)
            rms_xT()
            ffn()
            s5()
            rms_xT()
            ffn()
            rms_xT(for_dve=True)
            pool()
            rms_xT()
            ffn()
            rms_xT()
            fox(1)
            rms_xT()
            ffn()
            def plain_xT():
                pe.wait_ge(x_ready, t.value("x_ready"))
                xT_ready(turn(x))

            def hybrid(l):
                pe.wait_ge(x_ready, t.value("x_ready"))
                xT_ready(turn(x))
                slot, w = wslot(512)
                claim(4, 5)
                for m in range(4):
                    ins = feats(ps[:, 4 + m // 2, (m % 2) * S:(m % 2 + 1) * S], w, m * P, P, xT)
                release(slot)
                tk = to_act(ins, 4, 5)
                slot, w = wslot(512)
                for i in range(TT):
                    claim(6 + i)
                    rv_tk = to_act(rows(ps[:, 6 + i, :], xT, i, w, 0, 512), 6 + i)
                release(slot)
                pe.wait_ge(*tk)
                claim(0, 1)
                for c in range(2):
                    ins = pe.matmul(ps[:, c, :], lhsT=cst("ret_swap"),
                                    rhs=r_qk[:, 2 * c:2 * c + 2, :].rearrange("p a n -> p (a n)"), start=True, stop=True)
                    if c == 0:
                        carry(ins)
                to_dve(ins, 0, 1)
                slot, w = wslot(512)
                claim(2, 3)
                for m in range(4):
                    ins = feats(ps[:, 2 + m // 2, (m % 2) * S:(m % 2 + 1) * S], w, m * P, P, xT)
                to_dve(ins, 2, 3)
                release(slot)
                slot, w = wslot(520)
                for i in range(TT):
                    claim(4 + i)
                    to_act(rows(ps[:, 4 + i, :], xT, i, w, 0, 512), 4 + i)
                claim(6)
                for a in range(2):
                    ins = feats(ps[0:4, 6, a * S:(a + 1) * S], w, 512 + 4 * a, 4, xT)
                mo_tk = to_act(ins, 6)
                release(slot)
                pe.wait_ge(dve_to_pe, t.up("dve_to_pe"))

                def scores_T(b0, p, q, k):
                    claim(b0, b0 + 1)
                    for r in range(2):
                        pr = slice(HD * r, HD * r + HD)
                        carry(pe.matmul(ps[:, b0 + r, 0:S], lhsT=k[pr, p, 0:P], rhs=q[pr, p, :], start=True, stop=True))
                        ins = pe.matmul(ps[:, b0 + r, S:3 * P], lhsT=k[pr, p, P:S], rhs=q[pr, p, P:S], start=True, stop=True)
                    to_dve(ins, b0, b0 + 1)

                def weighted(outs, p, v_of):
                    pe.wait_ge(dve_to_pe, t.up("dve_to_pe"))
                    for r in range(2):
                        h = 2 * p + r
                        wt = prob[:, p, r]
                        pe.matmul(outs(0, h), lhsT=wt[:, 0:P], rhs=v_of(0, h), start=True, stop=True)
                        pe.matmul(outs(1, h), lhsT=wt[:, P:S], rhs=v_of(0, h), start=True, stop=False)
                        ins = pe.matmul(outs(1, h), lhsT=wt[:, S:3 * P], rhs=v_of(1, h), start=False, stop=True)
                    return ins
                for p in range(2):
                    scores_T(2 * p, p, r_qk[:, 0:2, :], r_qk[:, 2:4, :])
                pe.wait_ge(*rv_tk)
                claim(4)
                for p in range(2):
                    ins = weighted(lambda i, h: ps[:, 4, i * S + h * HD:i * S + (h + 1) * HD], p,
                                   lambda i, h: r_v[:, i, h * HD:(h + 1) * HD])
                to_dve(ins, 4)
                pe.wait_ge(dve_to_pe, t.up("dve_to_pe"))
                claim(5)
                for i in range(TT):
                    ins = pe.transpose(ps[:, 5, 4 * i:4 * i + 4], gates[0:4, 6, i * P:(i + 1) * P], ident[0:4, 0:4])
                to_act(ins, 5)
                for p, b0 in ((0, 6), (1, 0)):
                    claim(b0, b0 + 1)
                    for r in range(2):
                        h = 2 * p + r
                        for c0, n, kt in ((0, S, 0), (S, P, 1)):
                            o = ps[:, b0 + r, c0:c0 + n]
                            pe.matmul(o, lhsT=gates[0:4, 4, kt * P:(kt + 1) * P],
                                      rhs=ident[0:4, h:h + 1].to_broadcast([4, n]), start=True, stop=False)
                            ins = pe.matmul(o, lhsT=ident[0:4, h:h + 1].to_broadcast([4, P]),
                                            rhs=gates[0:4, 5, S - n:S], start=False, stop=True)
                    to_dve(ins, b0, b0 + 1)
                pe.wait_ge(act_to_pe, t.up("act_to_pe"))
                for p, b0 in ((0, 2), (1, 6)):
                    scores_T(b0, p, m_qk[:, 0:2, :], m_qk[:, 2:4, :])
                slot, w = wslot(416)
                for i in range(TT):
                    claim(i)
                    to_act(rows(ps[:, i, 0:384], xT, i, w, 0, 384), i)
                claim(2)
                kr_tk = to_act(feats(ps[0:96, 2, 0:S], w, 320, 96, xT), 2)
                release(slot)
                pe.wait_ge(*mo_tk)
                claim(4, 5)
                for p in range(2):
                    ins = weighted(lambda i, h: ps[:, 4 + i, h * 65:(h + 1) * 65], p, lambda i, h: m_v[:, i, h, :])
                to_dve(ins, 4, 5)
                pe.wait_ge(dve_to_pe, t.up("dve_to_pe"))
                claim(6, 7)
                for c in range(3):
                    for i in range(TT):
                        ins = pe.transpose(ps[:, 6 + c // 2, (c % 2) * S + i * P:(c % 2) * S + (i + 1) * P],
                                           c_rows[:, i, c * P:(c + 1) * P], ident)
                        carry(ins) if c == i == 0 else None
                cT_tk = to_act(ins, 6, 7)
                pe.wait_ge(*kr_tk)
                claim(3)
                sw = cst("mla_swap")[64:96, 64:96]
                to_dve(pe.matmul(ps[64:96, 3, 0:S], lhsT=sw, rhs=kr_T[64:96, :], start=True, stop=True), 3)
                pe.wait_ge(*cT_tk)
                slot, w = wslot(768, kt=2)
                q_tks = []
                for n, b in enumerate((0, 1, 2, 4)):
                    claim(b)
                    for a in range(2):
                        ins = feats(ps[0:96, b, a * S:(a + 1) * S], w, (2 * n + a) * 96, 96, cT, kt=2)
                    q_tks.append(to_act(ins, b))
                release(slot)
                pe.wait_ge(dve_to_pe, t.up("dve_to_pe"))
                claim(5, 6)
                for c in range(4):
                    for i in range(TT):
                        a = (c // 2) * 8 + i * 4 + (c % 2) * 2
                        ins = pe.transpose(ps[:, 5 + c // 2, (c % 2) * S + i * P:(c % 2) * S + (i + 1) * P],
                                           hn[:, a:a + 2, :].rearrange("p a n -> p (a n)"), ident)
                        carry(ins) if c == i == 0 else None
                to_act(ins, 5, 6)
                for n, b in enumerate((7, 3, 5, 6)):
                    pe.wait_ge(*q_tks[n])
                    claim(b)
                    to_dve(pe.matmul(ps[64:96, b, :], lhsT=sw,
                                     rhs=q_mla[64:96, 2 * n:2 * n + 2, :].rearrange("p a n -> p (a n)"), start=True,
                                     stop=True), b)
                slot, w = wslot(D, kt=1)
                for n, b in enumerate((0, 1, 2, 4)):
                    claim(b)
                    for a in range(2):
                        ins = feats(ps[0:HD, b, a * S:(a + 1) * S], w, (2 * n + a) * P, HD, cT[:, 2:3, :], kt=1)
                    tk = to_act(ins, b)
                wv = w[:, 0, :].rearrange("p (h e) -> p h e", e=P)[:, :, HD:P]
                for i in range(TT):
                    b = (7, 3)[i]
                    claim(b)
                    to_dve(pe.matmul(ps[:, b, :].rearrange("p (h e) -> p h e", e=HD), lhsT=cT[:, 2, i * P:(i + 1) * P],
                                     rhs=wv, start=True, stop=True), b)
                release(slot)
                pe.wait_ge(*tk)
                pe.wait_ge(dve_to_pe, t.up("dve_to_pe"))

                def score(i, r, o, q0, n):
                    h = 2 * i + r
                    return carry(pe.matmul(o, lhsT=q_mla[0:96, h, q0:q0 + P], rhs=k_mla[0:96, h, 0:n], start=True, stop=True))

                attend(4, score, lambda i, r, kt: v_mla[:, kt, (2 * i + r) * HD:(2 * i + r + 1) * HD])
                mix_out(plain=False)
                t.up("x_ready")

            t.up("x_ready")
            hybrid(0)
            plain_xT()
            ffn(plain=False)
            t.up("x_ready")
            hybrid(1)
            def moe_pass():
                pe.wait_ge(dve_to_pe, t.up("dve_to_pe"))
                claim(*range(8))
                for e in range(N_EXP):
                    for i in range(TT):
                        ins = pe.transpose(ps[0:CAP, 2 + e // 2, (e % 2) * S + i * P:(e % 2) * S + (i + 1) * P],
                                           perm_w[:, e, i, :], ident)
                gate_tk = to_dve(ins, 2, 3, 4, 5)

                def gather(e):
                    claim(6, 7)
                    for k in range(KD):
                        for i in range(TT):
                            ins = pe.matmul(ps[:, 6 + k // 4, (k % 4) * CAP:(k % 4 + 1) * CAP],
                                            lhsT=x[:, i, k * P:(k + 1) * P], rhs=perm[:, e, i, :],
                                            start=(i == 0), stop=(i == TT - 1))
                    return to_act(ins, 6, 7)

                xe_tk = gather(0)
                for e in range(N_EXP):
                    pe.wait_ge(*xe_tk)
                    claim(0, 1, 4, 5)
                    for b in (4, 5):
                        pe.matmul(ps[0:CAP, b, :], lhsT=zeros[0:1, 0:CAP], rhs=zeros[0:1, :], start=True, stop=False,
                                  skip_group_check=True)
                    slots = []

                    def gate_up():
                        slot = take()
                        slots.append(slot)
                        par = t.count["chunk"] % 2
                        t.up("chunk")
                        for half in range(2):
                            w = ring[:, slot, half * 2048:(half + 1) * 2048].rearrange("p (k n) -> p k n", n=FC)
                            for s in range(NSUB):
                                c0 = half * 256 + s * CAP
                                ins = feats(ps[:, par, c0:c0 + CAP], w, s * P, P, xe)
                        ins.then_inc(gate_full, 1)

                    def down(last=False):
                        slot = slots[-1] if last else slots[-2]
                        par = (t.count["hid_ready"] - 1) % 2
                        pe.wait_ge(hid_ready, t.up("hid_ready"))
                        w = ring[:, slot, 4096:6144].rearrange("p (s n) -> p s n", n=D)
                        for s in range(NSUB):
                            for c in range(2):
                                ins = pe.matmul(ps[0:CAP, 4 + c, :], lhsT=hid[:, par, s * CAP:(s + 1) * CAP],
                                                rhs=w[:, s, c * 512:(c + 1) * 512], start=False, stop=False,
                                                skip_group_check=True)
                        ins.then_inc(released[slot], 1)

                    gate_up()
                    with pe.Fori(0, M_ROUNDS) as i:
                        adds = {f"loaded{j}": 48 for j in range(RING)}
                        adds.update(chunk=RING, hid_ready=RING)
                        t.enter(i, M_ROUNDS, adds)
                        for _ in range(RING):
                            gate_up()
                            down()
                        t.leave()
                    for _ in range(M_LEFT):
                        gate_up()
                        down()
                    down(last=True)
                    for b in (4, 5):
                        ins = pe.matmul(ps[0:CAP, b, :], lhsT=zeros[0:1, 0:CAP], rhs=zeros[0:1, :], start=False, stop=True,
                                        skip_group_check=True)
                    y_tk = to_act(ins, 4, 5)
                    if e < N_EXP - 1:
                        xe_tk = gather(e + 1)
                    pe.wait_ge(*y_tk)
                    pe.wait_ge(*gate_tk)
                    for i in range(TT):
                        for c in range(2):
                            b = (2 + c, c)[i]
                            claim(b)
                            to_dve(pe.matmul(ps[:, b, :], lhsT=gate_T[0:CAP, e, i * P:(i + 1) * P],
                                             rhs=y_e[0:CAP, c * 512:(c + 1) * 512], start=True, stop=True), b)

            plain_xT()
            pe.wait_ge(router_loaded, 16)
            claim(4, 5)
            for i in range(TT):
                for k in range(KD):
                    ins = pe.matmul(ps[:, 4, i * N_EXP:(i + 1) * N_EXP], lhsT=xT[:, k, i * P:(i + 1) * P],
                                    rhs=router[:, k * N_EXP:(k + 1) * N_EXP], start=(k == 0), stop=(k == KD - 1))
            to_dve(ins, 4)
            pe.wait_ge(dve_to_pe, t.up("dve_to_pe"))
            sel = route[:, 5]
            pos = ps[:, 5, 0:3 * N_EXP].rearrange("p (a e) -> p a e", a=3)
            pe.matmul(pos[:, 0], lhsT=cst("before"), rhs=sel[:, 0], start=True, stop=True)
            pe.matmul(pos[:, 1], lhsT=cst("ones"), rhs=sel[:, 0], start=True, stop=False)
            pe.matmul(pos[:, 1], lhsT=cst("before"), rhs=sel[:, 1], start=False, stop=True)
            pe.matmul(pos[:, 2], lhsT=cst("ones"), rhs=sel[:, 0], start=True, stop=False)
            to_dve(pe.matmul(pos[:, 2], lhsT=cst("ones"), rhs=sel[:, 1], start=False, stop=True), 5)
            moe_pass()
            pe.wait_ge(overflow_ready, 1)
            more = pe.value_load(overflow[0:1, 0:1], min_val=0, max_val=1)
            with pe.If(more > 0):
                for _ in range(1, PASSES):
                    moe_pass()

        @block.vector
        def _(dve):
            t = Tally()

            def then(ins):
                ins.then_inc(dve_step, 1)
                dve.wait_ge(dve_step, t.up("dve_step"))

            def signal_op():
                c = t.up("marks") - 1
                return dve.memset(marks[:, c:c + 1], 0.0)

            def signal(which, n=1):
                signal_op().then_inc(which, n)

            def drain(ins):
                ins.then_inc(drained_dve, 1)
                return t.up("drained_dve")

            def full():
                dve.wait_ge(full_dve, t.up("full_dve"))

            def rms_xT(g):
                dve.wait_ge(act_to_dve, t.up("act_to_dve"))
                then(dve.reciprocal(small[:, 6:8], small[:, 4:6]))
                for i in range(TT):
                    ins = dve.tensor_scalar(xn[:, i, :], x[:, i, :], small[:, 6 + i:7 + i], None, ALU.mult)
                ins.then_inc(dve_to_pe, 1)
                xT_banks(g)

            def xT_banks(g):
                for j in (1, 3):
                    full()
                    for kk in range(2):
                        k = 2 * j + kk
                        if g is None:
                            ins = dve.tensor_copy(xT[:, k, :], ps[:, j, kk * S:(kk + 1) * S])
                        else:
                            ins = dve.tensor_scalar(xT[:, k, :], ps[:, j, kk * S:(kk + 1) * S], vec[:, g + k:g + k + 1],
                                                    None, ALU.mult)
                    drain(ins)

            def add_x(o, src, alpha):
                if alpha is None:
                    return dve.tensor_tensor(o, o, src, ALU.add)
                return dve.scalar_tensor_tensor(out=o, in0=o, scalar=alpha, in1=src, op0=ALU.mult, op1=ALU.add)

            def ffn(alpha=None, last=True):
                def one():
                    par = t.count.get("up_full", 0) % 2
                    dve.wait_ge(up_full, t.up("up_full"))
                    dve.wait_ge(silu_ready, t.up("silu_ready"))
                    dve.tensor_tensor(hid[:, par, :], silu[:, par, :], ps[:, 2 * par + 1, :], ALU.mult).then_inc(hid_ready, 1)
                one()
                with dve.Fori(0, ROUNDS) as i:
                    t.enter(i, ROUNDS, {"up_full": RING, "silu_ready": RING})
                    for _ in range(RING):
                        one()
                    t.leave()
                for _ in range(LEFT):
                    one()
                full()
                for i in range(TT):
                    for c in range(2):
                        ins = add_x(x[:, i, c * 512:(c + 1) * 512], ps[:, 4 + 2 * i + c, :], alpha)
                if alpha is None:
                    ins.then_inc(x_ready, 1)
                else:
                    drain(ins)

            def mix_out(alpha=None):
                for c in range(2):
                    for i in range(TT):
                        full()
                        ins = add_x(x[:, i, c * 512:(c + 1) * 512], ps[:, 2 * c + i, :], alpha)
                        if c == 1 and i == TT - 1 and alpha is None:
                            ins.then_inc(x_ready, 1)
                        else:
                            drain(ins)

            def fox(j):
                for c in (1, 0):
                    for i in range(TT):
                        full()
                        drain(dve.tensor_copy(v_rows[:, i, c * 512:(c + 1) * 512], ps[:, (1 if c else 3) + i, :]))
                dve.wait_ge(act_to_dve, t.up("act_to_dve"))
                then(dve.tensor_scalar(f_buf[0:16, 2, :], f_buf[0:16, 0, :], 0.0, None, ALU.min))
                then(dve.tensor_tensor(f_buf[0:16, 3, :], f_buf[0:16, 1, :], f_buf[0:16, 2, :], ALU.subtract))
                then(dve.memset(negC[:, :], 0.0))
                then(dve.tensor_tensor_scan(negC[0:16, :], cst("ones", 16, 0, 1).to_broadcast([16, S]), f_buf[0:16, 3, :],
                                            0.0, ALU.mult, ALU.add))
                dve.tensor_copy(negC[HD:HD + 16, :], negC[0:16, :]).then_inc(dve_to_pe, 1)
                for i in range(4):
                    full()
                    drain(dve.tensor_copy(kT[:, 2 * i:2 * i + 2, :], ps[:, (9 + i) % 8, :].rearrange("p (a b) -> p a b", b=S)))
                attend(8, "fox_mask", lambda i: mixT[:, i, :])
                mix_out()

            def attend(pairs, mask, o_of):
                m = cst(mask).unsqueeze(1).to_broadcast([P, 2, 3 * P])
                for i in range(pairs + 2):
                    if i < pairs:
                        par = i % 2
                        c = 16 + 8 * par
                        full()
                        ins = dve.tensor_tensor(prob[:, par, :, :], ps[:, 2 * par:2 * par + 2, 0:3 * P], m, ALU.add)
                        dve.wait_ge(drained_dve, drain(ins))
                        dve.tensor_reduce(small[:, c:c + 2], prob[:, par, :, 0:P], AX.X, ALU.max, negate=True)
                        dve.tensor_reduce(small[:, c + 2:c + 4], prob[:, par, :, P:3 * P], AX.X, ALU.max, negate=True)\
                           .then_inc(dve_to_act, 1)
                    if 1 <= i <= pairs:
                        par = (i - 1) % 2
                        c = 16 + 8 * par + 4
                        dve.wait_ge(act_to_dve, t.up("act_to_dve"))
                        then(dve.reciprocal(small[:, c:c + 4], small[:, c:c + 4]))
                        dve.tensor_tensor(prob[:, par, :, 0:P], prob[:, par, :, 0:P],
                                          small[:, c:c + 2].unsqueeze(2).to_broadcast([P, 2, P]), ALU.mult)
                        dve.tensor_tensor(prob[:, par, :, P:3 * P], prob[:, par, :, P:3 * P],
                                          small[:, c + 2:c + 4].unsqueeze(2).to_broadcast([P, 2, S]), ALU.mult)\
                           .then_inc(dve_to_pe, 1)
                    if i >= 2:
                        full()
                        drain(dve.tensor_copy(o_of(i - 2), ps[:, 6 + i % 2, 0:S]))

            def s5():
                dve.wait_ge(s5_loaded, S5_LOADS)
                dve.tensor_scalar(c_in[:, 1, :, 0:64], c_in[:, 0, :, 64:P], -1.0, None, ALU.mult)
                then(dve.tensor_scalar(c_in[:, 1, :, 64:P], c_in[:, 0, :, 0:64], -1.0, None, ALU.mult))
                dve.tensor_scalar(c_in[:, 0, :, 64:P], c_in[:, 0, :, 64:P], -1.0, None, ALU.mult).then_inc(dve_to_pe, 1)
                full()
                drain(dve.tensor_copy(s5p[:, 0:2, :], ps[:, 0, 0:2 * G5].rearrange("p (a g) -> p a g", a=2)))
                dve.wait_ge(drained_dve, t.value("drained_dve"))
                dve.wait_ge(act_to_dve, t.up("act_to_dve"))
                tt, ts = dve.tensor_tensor, dve.tensor_scalar
                then(tt(t0, a_re, dt5, ALU.mult))
                then(tt(t1, a_im, dt5, ALU.mult))
                then(ts(t2, t1, 1.0 / (2 * np.pi), MAGIC, ALU.mult, ALU.add))
                then(ts(t2, t2, MAGIC, None, ALU.subtract))
                then(dve.scalar_tensor_tensor(out=t1, in0=t2, scalar=-TWO_PI_HI, in1=t1, op0=ALU.mult, op1=ALU.add))
                then(dve.scalar_tensor_tensor(out=t1, in0=t2, scalar=-TWO_PI_LO, in1=t1, op0=ALU.mult, op1=ALU.add))
                ts(t1, t1, 3.1415925, -3.1415925, ALU.min, ALU.max).then_inc(dve_to_act, 1)
                dve.wait_ge(act_to_dve, t.up("act_to_dve"))
                then(ts(phi_hi, t1, 4096.0 / (2 * np.pi), MAGIC, ALU.mult, ALU.add))
                then(ts(phi_hi, phi_hi, MAGIC, 1.0 / 4096, ALU.subtract, ALU.mult))
                then(dve.scalar_tensor_tensor(out=phi_lo, in0=t1, scalar=1.0 / (2 * np.pi), in1=phi_hi, op0=ALU.mult,
                                              op1=ALU.subtract))
                then(tt(t2, t2, t2, ALU.mult))
                then(ts(t2, t2, -2.0, 1.0, ALU.mult, ALU.add))
                then(tt(t2, mag, t2, ALU.mult))
                then(ts(t2, t2, 1.0, None, ALU.subtract))
                then(tt(t3, mag, t3, ALU.mult))
                then(tt(t0, a_re, a_re, ALU.mult))
                then(tt(t1, a_im, a_im, ALU.mult))
                then(tt(t0, t0, t1, ALU.add))
                then(dve.reciprocal(t0, t0))
                then(tt(k_re, t2, a_re, ALU.mult))
                then(tt(t1, t3, a_im, ALU.mult))
                then(tt(k_re, k_re, t1, ALU.add))
                then(tt(k_re, k_re, t0, ALU.mult))
                then(tt(k_im, t3, a_re, ALU.mult))
                then(tt(t1, t2, a_im, ALU.mult))
                then(tt(k_im, k_im, t1, ALU.subtract))
                then(tt(k_im, k_im, t0, ALU.mult))
                then(ts(t2, k_im, cst("half_sign"), None, ALU.mult))
                then(ts(t3, k_re, cst("half_sign"), -1.0, ALU.mult, ALU.mult))
                tmp = uT.rearrange("p a b -> p (a b)")[:, 0:G5 * C5].rearrange("p (g c) -> p g c", c=C5)

                def wide(v):
                    return v.unsqueeze(2).to_broadcast([P, G5, C5])
                then(tt(bb, wide(k_re), b_own, ALU.mult))
                then(tt(tmp, wide(t2), b_other, ALU.mult))
                then(tt(bb, bb, tmp, ALU.add))
                then(tt(bb_turn, wide(k_im), b_own, ALU.mult))
                then(tt(tmp, wide(t3), b_other, ALU.mult))
                tt(bb_turn, bb_turn, tmp, ALU.add).then_inc(dve_to_pe, 1)
                full()
                drain(dve.tensor_copy(c_T.rearrange("p a k n -> p (a k n)").rearrange("p (b n) -> p b n", b=4), ps[:, 1:5, :]))
                full()
                dve.tensor_copy(bT.rearrange("p a k n -> p (a k n)")[:, 0:1536].rearrange("p (b n) -> p b n", b=3), ps[:, 5:8, :])
                drain(dve.tensor_copy(bT.rearrange("p a k n -> p (a k n)")[:, 1536:2048], ps[:, 0, :]))
                dve.memset(c_pad[:, :, :, :], 0.0).then_inc(bu_done, 2)
                signal(sin_ready, 2)
                signal(z_ready, 2)
                rms_xT(VEC_AT["mix_norm_g"] + KD)
                signal(dve_to_act, 1)

                def step(ins, T, k):
                    ins.then_inc(dve_loop_step, 1)
                    dve.wait_ge(dve_loop_step, T * (3 * GPT + 1) + k)

                with dve.Fori(0, 8) as T:
                    for a in range(2):
                        at = c_pad_at + a * 1024
                        dst = arena[:, at:at + 8 * 144].rearrange("p (g n) -> p g n", n=144)[:, :, 0:C5]
                        ins = dve.tensor_copy(dst, c_T[:, a, bass.ds(T, 1), :].squeeze(1).rearrange("p (g c) -> p g c", c=C5))
                    ins.then_inc(c_pad_ready, 1)
                    for j in range(GPT):
                        par = j % 2
                        g = bass.ds(T * GPT + j, 1)
                        dve.wait_ge(bu_done, T * GPT + (j + 3))
                        dve.wait_ge(sin_ready, T * GPT + (j + 3))
                        dve.tensor_tensor(w5[:, 0, :], ps[:, par, 0:S], rot[:, 2 + par, :], ALU.mult)
                        step(dve.tensor_tensor(w5[:, 1, :], ps[:, par, S:2 * S], rot[:, par, :], ALU.mult), T, 3 * j + 1)
                        step(dve.tensor_tensor(w5[:, 0, :], w5[:, 0, :], w5[:, 1, :], ALU.add), T, 3 * j + 2)
                        step(dve.tensor_tensor_scan(z_one, mag[:, g].to_broadcast([P, S]), w5[:, 0, :], 0.0, ALU.mult,
                                                    ALU.add), T, 3 * j + 3)
                        dve.tensor_tensor(zr(par, 0), z_one, rot[:, 2 + par, :], ALU.mult)
                        dve.tensor_tensor(zr(par, 1), z_one, rot[:, par, :], ALU.mult).then_inc(z_ready, 1)
                    dve.wait_ge(y_full, T + 1)
                    step(dve.scalar_tensor_tensor(out=gT[:, bass.ds(T, 1), :].squeeze(1), in0=uT[:, bass.ds(T, 1), :].squeeze(1),
                                                  scalar=vec[:, bass.ds(T + VEC_AT["s5_d"], 1)], in1=ps[:, 6, 0:S],
                                                  op0=ALU.mult, op1=ALU.add), T, 3 * GPT + 1)
                signal(dve_to_act, 1)
                for c in range(2):
                    for i in range(TT):
                        full()
                        dve.wait_ge(act_to_dve, t.up("act_to_dve"))
                        b = 4 * c + i
                        dve.wait_ge(drained_dve, drain(tt(glu[:, 2 * c + i, :], glu[:, 2 * c + i, :], ps[:, b, :], ALU.mult)))
                        xs = x[:, i, c * 512:(c + 1) * 512]
                        ins = tt(xs, xs, glu[:, 2 * c + i, :], ALU.add)
                ins.then_inc(x_ready, 1)

            def pool():
                for g, w in enumerate(WINDOWS):
                    src = xT[:, 2 * g:2 * g + 2, :]
                    cur, sh = src, 1
                    while sh < w:
                        nxt = pool_s[:, (sh.bit_length() - 1) % 2, :, :]
                        dve.tensor_copy(nxt[:, :, 0:sh], cur[:, :, 0:sh])
                        then(dve.tensor_tensor(nxt[:, :, sh:S], cur[:, :, sh:S], cur[:, :, 0:S - sh], ALU.add))
                        cur, sh = nxt, 2 * sh
                    then(dve.tensor_tensor(cur, cur, cst(f"pool{w}").unsqueeze(1).to_broadcast([P, 2, S]), ALU.mult))
                    ins = dve.tensor_tensor(mixT[:, 2 * g:2 * g + 2, :], cur, src, ALU.subtract)
                    if g < len(WINDOWS) - 1:
                        then(ins)
                ins.then_inc(dve_to_pe, 1)
                dve.wait_ge(rows_loaded, t.up("rows_loaded", 32))
                for i in range(TT):
                    for c in range(2):
                        cs = slice(c * 512, (c + 1) * 512)
                        full()
                        o = row_tmp[:, i, cs]
                        dve.wait_ge(drained_dve, drain(dve.tensor_tensor(o, ps[:, 2 * i + c, :], rowv[:, 0, cs], ALU.add)))
                        then(dve.tensor_tensor(o, o, rowv[:, 1, cs], ALU.mult))
                        ins = dve.tensor_tensor(x[:, i, cs], x[:, i, cs], o, ALU.add)
                ins.then_inc(x_ready, 1)

            dve.memset(zeros[:, :], 0.0).then_inc(hid_ready, 1)
            dve.wait_ge(x_loaded, 16)
            dve.wait_ge(const_loaded, 16)
            then(dve.memset(small[:, :], 0.0))
            dve.memset(eps1, EPS1)
            dve.memset(eps2, EPS2)
            dve.memset(one, 1.0).then_inc(x_ready, 1)
            full()
            drain(dve.tensor_copy(vec[:, 0:VEC_TOTAL], ps[:, 7, 0:VEC_TOTAL]))
            rms_xT(VEC_AT["mix_norm_g"])
            fox(0)
            rms_xT(VEC_AT["ffn_norm_g"])
            ffn()
            s5()
            rms_xT(VEC_AT["ffn_norm_g"] + KD)
            ffn()
            rms_xT(VEC_AT["mix_norm_g"] + 2 * KD)
            dve.wait_ge(act_to_dve, t.up("act_to_dve"))
            pool()
            rms_xT(VEC_AT["ffn_norm_g"] + 2 * KD)
            ffn()
            rms_xT(VEC_AT["mix_norm_g"] + 3 * KD)
            fox(1)
            rms_xT(VEC_AT["ffn_norm_g"] + 3 * KD)
            ffn()
            def ln():
                for i in range(TT):
                    for c in range(2):
                        ins = dve.bn_stats(small[:, 48 + 6 * c:54 + 6 * c], x[:, i, c * 512:(c + 1) * 512])
                    then(ins)
                    then(dve.bn_aggr(small[:, 60:62], small[:, 48:60]))
                    dve.tensor_copy(small[:, 42 + i:43 + i], small[:, 60:61])
                    ins = dve.tensor_copy(small[:, 44 + i:45 + i], small[:, 61:62])
                ins.then_inc(dve_to_act, 1)
                dve.wait_ge(act_to_dve, t.up("act_to_dve"))
                then(dve.reciprocal(small[:, 6:8], small[:, 4:6]))
                dve.wait_ge(rows_loaded, t.up("rows_loaded", 32))
                for i in range(TT):
                    then(dve.tensor_scalar(x[:, i, :], x[:, i, :], small[:, 42 + i:43 + i], small[:, 6 + i:7 + i],
                                           ALU.subtract, ALU.mult))
                    then(dve.tensor_tensor(x[:, i, :], x[:, i, :], rowv[:, 0, :], ALU.mult))
                    ins = dve.tensor_tensor(x[:, i, :], x[:, i, :], rowv[:, 1, :], ALU.add)
                ins.then_inc(x_ready, 1)

            def last_ln():
                def then(ins):
                    ins.then_inc(late_step, 1)
                    dve.wait_ge(late_step, t.up("late_step"))
                then(signal_op())
                for i in range(TT):
                    for c in range(2):
                        ins = dve.bn_stats(small[:, 48 + 6 * c:54 + 6 * c], acc[:, i, c * 512:(c + 1) * 512])
                    then(ins)
                    then(dve.bn_aggr(small[:, 60:62], small[:, 48:60]))
                    dve.tensor_copy(small[:, 42 + i:43 + i], small[:, 60:61])
                    ins = dve.tensor_copy(small[:, 44 + i:45 + i], small[:, 61:62])
                ins.then_inc(late_to_act, 1)
                dve.wait_ge(late_to_dve, 1)
                then(dve.reciprocal(small[:, 6:8], small[:, 4:6]))
                dve.wait_ge(rows_loaded, t.up("rows_loaded", 32))
                for i in range(TT):
                    then(dve.tensor_scalar(x[:, i, :], acc[:, i, :], small[:, 42 + i:43 + i], small[:, 6 + i:7 + i],
                                           ALU.subtract, ALU.mult))
                    then(dve.tensor_tensor(x[:, i, :], x[:, i, :], rowv[:, 0, :], ALU.mult))
                    ins = dve.tensor_tensor(x[:, i, :], x[:, i, :], rowv[:, 1, :], ALU.add)
                ins.then_inc(x_ready, 1)

            def final_norm():
                dve.wait_ge(act_to_dve, t.up("act_to_dve"))
                then(dve.reciprocal(small[:, 6:8], small[:, 4:6]))
                dve.wait_ge(rows_loaded, t.up("rows_loaded", 16))
                for i in range(TT):
                    ins = dve.scalar_tensor_tensor(out=x[:, i, :], in0=x[:, i, :], scalar=small[:, 6 + i:7 + i],
                                                   in1=rowv[:, 0, :], op0=ALU.mult, op1=ALU.mult)
                ins.then_inc(x_ready, 1)

            def hybrid(l):
                tt, ts = dve.tensor_tensor, dve.tensor_scalar
                stt = dve.scalar_tensor_tensor
                xT_banks(None)
                full()
                ta = tmp_a.rearrange("p (a n) -> p a n", a=4)
                dve.wait_ge(drained_dve, drain(tt(ta, ps[:, 0:2, :].rearrange("p b (a n) -> p (b a) n", a=2),
                                                  cst("ret_sin").unsqueeze(1).to_broadcast([P, 4, S]), ALU.mult)))
                then(tt(r_qk, r_qk, cst("ret_cos").unsqueeze(1).to_broadcast([P, 4, S]), ALU.mult))
                tt(r_qk, r_qk, ta, ALU.add).then_inc(dve_to_pe, 1)
                full()
                for c in range(4):
                    src = ps[:, 2 + c // 2, (c % 2) * S:(c % 2 + 1) * S]
                    def wc(tap):
                        return v_col("mlstm_conv_w_2", l * 16 + tap * 4 + c)
                    ins = ts(m_qk[:, c, :], src, wc(3), v_col("mlstm_conv_b_2", l * 4 + c), ALU.mult, ALU.add)
                    for j in (1, 2, 3):
                        then(ins)
                        ins = stt(out=m_qk[:, c, j:S], in0=src[:, 0:S - j], scalar=wc(3 - j), in1=m_qk[:, c, j:S],
                                  op0=ALU.mult, op1=ALU.add)
                    if c < 3:
                        then(ins)
                dve.wait_ge(drained_dve, drain(ins))
                dve.wait_ge(act_to_dve, t.up("act_to_dve"))
                g = gates[0:4]
                dve.memset(m_v[:, :, :, HD:HD + 1], 1.0).then_inc(dve_to_act, 1)
                then(ts(g[:, 7, :], g[:, 1, :], 0.0, None, ALU.min))
                then(tt(g[:, 7, :], g[:, 2, :], g[:, 7, :], ALU.subtract))
                then(dve.tensor_tensor_scan(g[:, 3, :], cst("ones", 4, 0, 1).to_broadcast([4, S]), g[:, 7, :], 0.0,
                                            ALU.mult, ALU.add))
                then(tt(g[:, 4, :], g[:, 0, :], g[:, 3, :], ALU.add))
                then(dve.tensor_tensor_scan(g[:, 7, :], g[:, 4, :], g[:, 4, :], NEG, ALU.max, ALU.max))
                then(ts(g[:, 5, :], g[:, 7, :], -1.0, None, ALU.mult))
                then(tt(g[:, 6, :], g[:, 3, :], g[:, 7, :], ALU.subtract))
                for p in range(2):
                    full()
                    ins = tt(prob[:, p], ps[:, 2 * p:2 * p + 2, 0:3 * P],
                             cst("ret_decay", P, 2 * p * 384, 768).rearrange("p (a n) -> p a n", a=2), ALU.mult)
                    ins = drain_and(ins)
                    signal(dve_to_pe, 1)
                full()
                drain(dve.tensor_copy(hn[:, 0:8, :], ps[:, 4, :].rearrange("p (a n) -> p a n", n=HD)))
                signal(dve_to_pe, 1)
                mm = cst("mlstm_mask").unsqueeze(1).to_broadcast([P, 2, 3 * P])
                for p, b0 in ((0, 6), (1, 0)):
                    full()
                    drain_and(tt(probT[:, p], ps[:, b0:b0 + 2, 0:3 * P], mm, ALU.add))
                    signal(dve_to_act, 1)
                for p, b0 in ((0, 2), (1, 6)):
                    full()
                    dve.wait_ge(act_to_dve, t.up("act_to_dve"))
                    drain_and(stt(out=prob[:, p], in0=ps[:, b0:b0 + 2, 0:3 * P], scalar=HD ** -0.5, in1=probT[:, p],
                                  op0=ALU.mult, op1=ALU.mult))
                    signal(dve_to_pe, 1)
                dve.wait_ge(act_to_dve, t.up("act_to_dve"))
                then(dve.reciprocal(vec_ml[:, 12:16], vec_ml[:, 12:16]))
                for i in range(TT):
                    ts(c_rows[:, i, 0:S], c_rows[:, i, 0:S], vec_ml[:, 12 + i:13 + i], None, ALU.mult)
                    ins = ts(c_rows[:, i, S:384], c_rows[:, i, S:384], vec_ml[:, 14 + i:15 + i], None, ALU.mult)
                then(ins)
                full()
                for i in range(TT):
                    den = ps[:, 4 + i, 0:260].rearrange("p (h n) -> p h n", n=65)[:, :, HD:HD + 1].squeeze(2)
                    then(ts(vec_ml[:, 16 + 4 * i:20 + 4 * i], den, -1.0, None, ALU.mult))
                    then(tt(vec_ml[:, 16 + 4 * i:20 + 4 * i], vec_ml[:, 16 + 4 * i:20 + 4 * i], den, ALU.max))
                    then(tt(vec_ml[:, 16 + 4 * i:20 + 4 * i], vec_ml[:, 16 + 4 * i:20 + 4 * i],
                            vec_ml[:, 4 * i:4 * i + 4], ALU.max))
                    then(dve.reciprocal(vec_ml[:, 24 + 4 * i:28 + 4 * i], vec_ml[:, 16 + 4 * i:20 + 4 * i]))
                    num = ps[:, 4 + i, 0:260].rearrange("p (h n) -> p h n", n=65)[:, :, 0:HD]
                    ins = tt(hn[:, 8 + 4 * i:12 + 4 * i, :], num,
                             vec_ml[:, 24 + 4 * i:28 + 4 * i].unsqueeze(2).to_broadcast([P, 4, HD]), ALU.mult)
                    if i == 0:
                        then(ins)
                    else:
                        drain_and(ins)
                signal(dve_to_pe, 1)
                h8 = hn[:, 8:16, :].rearrange("p (i h) n -> p i (h n)", i=2)
                then(tt(h8, h8, m_o, ALU.mult))
                m16, v16 = vec_ml[:, 48:64], vec_ml[:, 32:48]
                ta = tmp_a.rearrange("p (a n) -> p a n", a=16)

                def wide(v):
                    return v.unsqueeze(2).to_broadcast([P, 16, HD])
                then(dve.tensor_reduce(m16, hn, AX.X, ALU.add))
                then(ts(m16, m16, 1.0 / HD, None, ALU.mult))
                then(tt(hn, hn, wide(m16), ALU.subtract))
                then(tt(ta, hn, hn, ALU.mult))
                dve.tensor_reduce(v16, ta, AX.X, ALU.add).then_inc(dve_to_act, 1)
                dve.wait_ge(act_to_dve, t.up("act_to_dve"))
                then(dve.reciprocal(v16, v16))
                then(tt(hn, hn, wide(v16), ALU.mult))
                h0 = hn[:, 0:8, :].rearrange("p (i h) n -> p i (h n)", i=2)
                tt(h0, h0, r_g, ALU.mult).then_inc(dve_to_pe, 1)
                cos, sin = cst("mla_cos")[64:96], cst("mla_sin")[64:96]
                full()
                kt_ = tmp_a[64:96, 0:S]
                drain_and(tt(kt_, ps[64:96, 3, 0:S], sin, ALU.mult))
                then(tt(kr_T[64:96, :], kr_T[64:96, :], cos, ALU.mult))
                then(tt(kt_, kt_, kr_T[64:96, :], ALU.add))
                dve.tensor_copy(k_mla[64:96, :, :], kt_.unsqueeze(1).to_broadcast([32, 8, S]))
                for n, b in enumerate((7, 3, 5, 6)):
                    full()
                    o = q_mla[64:96, 2 * n:2 * n + 2, :]
                    qt = tmp_a[64:96, 256 + 0:768].rearrange("p (a n) -> p a n", a=2)
                    drain_and(tt(qt, ps[64:96, b, :].rearrange("p (a n) -> p a n", a=2),
                                 sin.unsqueeze(1).to_broadcast([32, 2, S]), ALU.mult))
                    then(tt(o, o, cos.unsqueeze(1).to_broadcast([32, 2, S]), ALU.mult))
                    then(tt(o, o, qt, ALU.add))
                for i in range(TT):
                    full()
                    drain(dve.tensor_copy(v_mla[:, i, :], ps[:, (7, 3)[i], :]))
                signal(dve_to_pe, 1)
                attend(4, "mla_mask", lambda i: mixT[:, 2 + i, :])
                mix_out(alpha=DN_ALPHA)
                dve.wait_ge(drained_dve, t.value("drained_dve"))

            def drain_and(ins):
                dve.wait_ge(drained_dve, drain(ins))

            final_norm()
            hybrid(0)
            ln()
            xT_banks(None)
            ffn(alpha=DN_ALPHA)
            dve.wait_ge(drained_dve, t.value("drained_dve"))
            ln()
            hybrid(1)
            ln()
            def moe_pass(b):
                if b > 0:
                    then(dve.tensor_scalar(route[:, 7], route[:, 7], float(CAP), None, ALU.subtract))
                for e in range(N_EXP):
                    for i in range(TT):
                        place = cst("tokens", P, 0, CAP)
                        dve.tensor_scalar(perm[:, e, i, :], place, route[:, 7, i, e:e + 1], None, ALU.is_equal)
                        ins = dve.tensor_scalar(perm_w[:, e, i, :], place, route[:, 7, i, e:e + 1],
                                                route[:, 6, i, e:e + 1], ALU.is_equal, ALU.mult)
                ins.then_inc(dve_to_pe, 1)
                full()
                drain(dve.tensor_copy(gate_T[0:CAP].rearrange("p e n -> p (e n)").rearrange("p (b n) -> p b n", b=4),
                                      ps[0:CAP, 2:6, :]))
                for e in range(N_EXP):
                    def one():
                        par = t.count["silu_ready"] % 2
                        dve.wait_ge(silu_ready, t.up("silu_ready"))
                        dve.tensor_tensor(hid[:, par, 0:NSUB * CAP], silu[:, par, 0:NSUB * CAP],
                                          ps[:, par, 256:256 + NSUB * CAP], ALU.mult).then_inc(hid_ready, 1)
                    one()
                    with dve.Fori(0, M_ROUNDS) as i:
                        t.enter(i, M_ROUNDS, {"silu_ready": RING})
                        for _ in range(RING):
                            one()
                        t.leave()
                    for _ in range(M_LEFT):
                        one()
                    for i in range(TT):
                        for c in range(2):
                            full()
                            o = acc[:, i, c * 512:(c + 1) * 512]
                            drain(dve.tensor_tensor(o, o, ps[:, (2 + c, c)[i], :], ALU.add))

            xT_banks(None)
            for i in range(TT):
                dve.tensor_scalar(acc[:, i, :], x[:, i, :], DN_ALPHA, None, ALU.mult)
            lg, mx, ixf, oh1, oh2, sel, gate, posm, wgt, dif = (route[:, i] for i in range(10))
            full()
            drain_and(dve.tensor_copy(lg, ps[:, 4, 0:TT * N_EXP].rearrange("p (i e) -> p i e", i=TT)))
            for i in range(TT):
                then(dve.max(mx[:, i, :], lg[:, i, :]))
                then(dve.max_index(route_idx[:, i, :], mx[:, i, :], lg[:, i, :]))
            dve.tensor_copy(ixf, route_idx[:, :, :])
            then(dve.memset(dif, 0.0))
            dve.tensor_tensor(dif[:, :, 0:1], mx[:, :, 1:2], mx[:, :, 0:1], ALU.subtract).then_inc(dve_to_act, 1)
            for i in range(TT):
                dve.tensor_scalar(oh1[:, i, :], cst("experts"), ixf[:, i, 0:1], None, ALU.is_equal)
                ins = dve.tensor_scalar(oh2[:, i, :], cst("experts"), ixf[:, i, 1:2], None, ALU.is_equal)
            then(ins)
            dve.tensor_tensor(sel, oh1, oh2, ALU.add).then_inc(dve_to_pe, 1)
            dve.wait_ge(act_to_dve, t.up("act_to_dve"))
            then(dve.tensor_scalar(wgt[:, :, 0:1], dif[:, :, 0:1], 1.0, None, ALU.add))
            then(dve.reciprocal(wgt[:, :, 0:1], wgt[:, :, 0:1]))
            then(dve.tensor_tensor(wgt[:, :, 1:2], dif[:, :, 0:1], wgt[:, :, 0:1], ALU.mult))
            for i in range(TT):
                then(dve.tensor_scalar(gate[:, i, :], oh2[:, i, :], wgt[:, i, 1:2], None, ALU.mult))
                then(dve.scalar_tensor_tensor(out=gate[:, i, :], in0=oh1[:, i, :], scalar=wgt[:, i, 0:1],
                                              in1=gate[:, i, :], op0=ALU.mult, op1=ALU.add))
            full()
            pos = ps[:, 5, 0:3 * N_EXP].rearrange("p (a e) -> p a e", a=3)
            then(dve.scalar_tensor_tensor(out=posm, in0=pos[:, 0:2], scalar=1.0, in1=sel, op0=ALU.add, op1=ALU.mult))
            then(dve.tensor_scalar(posm, posm, 1.0, None, ALU.subtract))
            drain_and(dve.tensor_reduce(small[:, 33:34], pos[:, 2], AX.X, ALU.max))
            then(dve.tensor_scalar(small[:, 34:35], small[:, 33:34], float(CAP), None, ALU.is_gt))
            dve.tensor_copy(overflow[:, :], small[:, 34:35]).then_inc(overflow_ready, 1)
            moe_pass(0)
            dve.wait_ge(overflow_ready, 1)
            more = dve.value_load(overflow[0:1, 0:1], min_val=0, max_val=1)
            with dve.If(more > 0):
                for b in range(1, PASSES):
                    moe_pass(b)
            last_ln()


def kernel(**inputs):
    import concourse.bacc as bacc
    from concourse.bass_utils import run_bass_kernel_spmd

    nc = bacc.Bacc("TRN2", target_bir_lowering=False, num_devices=1)
    arrays, args = {}, {}
    for name in _INS:
        a = np.ascontiguousarray(inputs[name])
        arrays[f"in_{name}"] = a
        args[name] = nc.dram_tensor(f"in_{name}", a.shape, mybir.dt.from_np(a.dtype), kind="ExternalInput").ap()
    _, table = constant_table()
    arrays["in_table"] = table
    table_ap = nc.dram_tensor("in_table", table.shape, F32, kind="ExternalInput").ap()
    out = nc.dram_tensor("out", (1, S, D), F32, kind="ExternalOutput").ap()
    build(nc, args, table_ap, out)
    r = run_bass_kernel_spmd(nc, [arrays], core_ids=[0])
    return r.results[0]["out"]
```
